# Optimizing a Trainium2 kernel written in Bass

```python
import math
import jax, jax.numpy as jnp
from jax import lax
import numpy as np

D_MODEL = 2048
BATCH = 1
SEQ = 256
DEPTH = 2

GRID_W = 64
CTX_LEN = 256
ROT_DIM = 64
ROPE_THETA = 10000.0
EPS = 1e-6
BLOCK_Q = 128

MLA_HEADS = 6
MLA_NOPE = 128
MLA_ROPE = ROT_DIM
MLA_V = 128
MLA_Q_RANK = 512
MLA_KV_RANK = 256
NA_HEADS = 5
NA_DIM = 128
WIN_H = 8
WIN_W = 16
DIFF_HEADS = 5
DIFF_QK = ROT_DIM
DIFF_V = 2 * DIFF_QK

MLA_W = MLA_HEADS * MLA_V
NA_W = NA_HEADS * NA_DIM
DIFF_W = DIFF_HEADS * DIFF_V
MIX = MLA_W + NA_W + DIFF_W

IN_SIZES = (MLA_Q_RANK, MLA_KV_RANK, MLA_ROPE,
            NA_W, NA_W, NA_W,
            DIFF_HEADS * 2 * DIFF_QK, DIFF_HEADS * 2 * DIFF_QK, DIFF_W,
            MIX)
IN_WIDTH = int(sum(IN_SIZES))
IN_SPLITS = tuple(int(s) for s in np.cumsum(IN_SIZES)[:-1])

kernel_name = 'hybrid_mla_natten_diff_dit'

def rms_norm(x, g):
    xf = x.astype(jnp.float32)
    y = xf * lax.rsqrt(jnp.mean(xf * xf, axis=-1, keepdims=True) + EPS)
    return (y * g.astype(jnp.float32)).astype(x.dtype)

def axial_rope_tables(n, dim, dtype):
    t = jnp.arange(n)
    row = (t // GRID_W).astype(jnp.float32)
    col = (t % GRID_W).astype(jnp.float32)
    half = dim // 2
    inv = 1.0 / (ROPE_THETA ** (jnp.arange(0, half, 2, dtype=jnp.float32) / half))
    ang_r = row[:, None] * inv[None]
    ang_c = col[:, None] * inv[None]
    ang = jnp.concatenate([ang_r, ang_r, ang_c, ang_c], axis=-1)
    return jnp.cos(ang).astype(dtype), jnp.sin(ang).astype(dtype)

def apply_axial_rope(t, cos, sin):
    q = t.shape[-1] // 4
    a1, a2, b1, b2 = t[..., :q], t[..., q:2 * q], t[..., 2 * q:3 * q], t[..., 3 * q:]
    rot = jnp.concatenate([-a2, a1, -b2, b1], axis=-1)
    return t * cos + rot * sin

def split_heads(t, h):
    return t.reshape(t.shape[:2] + (h, t.shape[-1] // h))

def sweep_query_blocks(fn, *qs):
    B, n = qs[0].shape[:2]
    nb = n // BLOCK_Q
    blocks = tuple(jnp.moveaxis(q.reshape((B, nb, BLOCK_Q) + q.shape[2:]), 1, 0) for q in qs)
    out = lax.map(lambda a: fn(*a), blocks)
    return jnp.moveaxis(out, 0, 1).reshape((B, n) + out.shape[3:])

def mla_queries(cq, q_norm, w_uq):
    q = split_heads(rms_norm(cq, q_norm) @ w_uq, MLA_HEADS)
    return q[..., :MLA_NOPE], q[..., MLA_NOPE:]

def mla_keys(ckv, kv_norm, w_ukv):
    kv = split_heads(rms_norm(ckv, kv_norm) @ w_ukv, MLA_HEADS)
    return kv[..., :MLA_NOPE], kv[..., MLA_NOPE:]

def mla_attend(qn, qr, kn, kr, v):
    s = jnp.einsum('bqhd,bkhd->bhqk', qn, kn) + jnp.einsum('bqhr,bkr->bhqk', qr, kr)
    p = jax.nn.softmax(s.astype(jnp.float32) * (MLA_NOPE + MLA_ROPE) ** -0.5, axis=-1)
    return jnp.einsum('bhqk,bkhd->bqhd', p.astype(v.dtype), v)

def dense_attend(q, k, v):
    s = jnp.einsum('bqhd,bkhd->bhqk', q, k).astype(jnp.float32) * q.shape[-1] ** -0.5
    p = jax.nn.softmax(s, axis=-1)
    return jnp.einsum('bhqk,bkhd->bqhd', p.astype(v.dtype), v)

def na_latent(q, k, v, kc, vc, rpb):
    B, n, H, d = q.shape
    rows = n // GRID_W
    kh = min(WIN_H, rows)
    kw = WIN_W
    qg = q.reshape(B, rows, GRID_W, H, d)
    kg = k.reshape(B, rows, GRID_W, H, d)
    vg = v.reshape(B, rows, GRID_W, H, d)
    cols = jnp.arange(GRID_W)
    col_idx = jnp.clip(cols - kw // 2, 0, GRID_W - kw)[:, None] + jnp.arange(kw)[None]
    col_off = col_idx - cols[:, None] + (WIN_W - 1)
    scale = d ** -0.5

    def row_block(r):
        rs = jnp.clip(r - kh // 2, 0, rows - kh)
        q_r = lax.dynamic_index_in_dim(qg, r, axis=1, keepdims=False)
        k_win = lax.dynamic_slice_in_dim(kg, rs, kh, axis=1)[:, :, col_idx]
        v_win = lax.dynamic_slice_in_dim(vg, rs, kh, axis=1)[:, :, col_idx]
        row_off = rs + jnp.arange(kh) - r + (WIN_H - 1)
        bias = rpb[:, row_off][:, :, col_off].transpose(0, 2, 1, 3)
        s_win = (jnp.einsum('bqhd,baqkhd->bhqak', q_r, k_win).astype(jnp.float32) * scale
                 + bias[None].astype(jnp.float32))
        s_ctx = jnp.einsum('bqhd,bchd->bhqc', q_r, kc).astype(jnp.float32) * scale
        p = jax.nn.softmax(jnp.concatenate([s_win.reshape(B, H, GRID_W, kh * kw), s_ctx], axis=-1), axis=-1)
        p = p.astype(v.dtype)
        p_win = p[..., :kh * kw].reshape(B, H, GRID_W, kh, kw)
        p_ctx = p[..., kh * kw:]
        return (jnp.einsum('bhqak,baqkhd->bqhd', p_win, v_win)
                + jnp.einsum('bhqc,bchd->bqhd', p_ctx, vc))

    out = lax.map(row_block, jnp.arange(rows))
    return jnp.moveaxis(out, 0, 1).reshape(B, n, H, d)

def diff_attend(q1, q2, k1, k2, v, lam):
    scale = DIFF_QK ** -0.5
    s1 = jnp.einsum('bqhd,bkhd->bhqk', q1, k1).astype(jnp.float32) * scale
    s2 = jnp.einsum('bqhd,bkhd->bhqk', q2, k2).astype(jnp.float32) * scale
    a = jax.nn.softmax(s1, axis=-1) - lam * jax.nn.softmax(s2, axis=-1)
    return jnp.einsum('bhqk,bkhd->bqhd', a.astype(v.dtype), v)

def diff_post(o, subln, lam_init):
    return rms_norm(o, subln) * (1.0 - lam_init)

def mix_out(o_mla, o_na, o_diff, g, w_out):
    B, n = g.shape[:2]
    y = jnp.concatenate([o_mla.reshape(B, n, MLA_W), o_na.reshape(B, n, NA_W),
                         o_diff.reshape(B, n, DIFF_W)], axis=-1) * jax.nn.silu(g)
    return y @ w_out

def setup_inputs(seed: int = 0) -> dict:
    key = jax.random.key(seed)
    ks = jax.random.split(key, 20)

    def nrm(k, shape, s):
        return jax.random.normal(k, shape, jnp.float32) * s

    L, D = DEPTH, D_MODEL
    return {
        'x': nrm(ks[0], (BATCH, SEQ, D), 1.0),
        'c': nrm(ks[1], (BATCH, D), 1.0),
        'ctx': nrm(ks[2], (BATCH, CTX_LEN, D), 1.0),
        'c_ctx': nrm(ks[3], (D,), 1.0),
        'w_ada': nrm(ks[4], (L, D, 3 * D), 0.5 * D ** -0.5),
        'b_ada': nrm(ks[5], (L, 3 * D), 0.01),
        'norm_pre': 1.0 + nrm(ks[6], (L, D), 0.02),
        'norm_post': 1.0 + nrm(ks[7], (L, D), 0.02),
        'w_in': nrm(ks[8], (L, D, IN_WIDTH), D ** -0.5),
        'mla_q_norm': 1.0 + nrm(ks[9], (L, MLA_Q_RANK), 0.02),
        'mla_kv_norm': 1.0 + nrm(ks[10], (L, MLA_KV_RANK), 0.02),
        'w_uq': nrm(ks[11], (L, MLA_Q_RANK, MLA_HEADS * (MLA_NOPE + MLA_ROPE)), MLA_Q_RANK ** -0.5),
        'w_ukv': nrm(ks[12], (L, MLA_KV_RANK, MLA_HEADS * (MLA_NOPE + MLA_V)), MLA_KV_RANK ** -0.5),
        'na_rpb': nrm(ks[13], (L, NA_HEADS, 2 * WIN_H - 1, 2 * WIN_W - 1), 0.1),
        'diff_lq1': nrm(ks[14], (L, DIFF_QK), 0.1),
        'diff_lk1': nrm(ks[15], (L, DIFF_QK), 0.1),
        'diff_lq2': nrm(ks[16], (L, DIFF_QK), 0.1),
        'diff_lk2': nrm(ks[17], (L, DIFF_QK), 0.1),
        'diff_subln': 1.0 + nrm(ks[18], (L, DIFF_V), 0.02),
        'w_out': nrm(ks[19], (L, MIX, D), MIX ** -0.5),
    }

def reference(x, c, ctx, c_ctx, w_ada, b_ada, norm_pre, norm_post, w_in, mla_q_norm, mla_kv_norm,
              w_uq, w_ukv, na_rpb, diff_lq1, diff_lk1, diff_lq2, diff_lk2, diff_subln, w_out):
    B, n, _ = x.shape
    C = ctx.shape[1]
    cos, sin = axial_rope_tables(n, ROT_DIM, x.dtype)
    cos_h, sin_h = cos[:, None, :], sin[:, None, :]
    cos_d, sin_d = cos[:, None, None, :], sin[:, None, None, :]
    hc = ctx
    for i in range(DEPTH):
        last = i == DEPTH - 1
        lam_init = 0.8 - 0.6 * math.exp(-0.3 * i)
        lam = (jnp.exp(jnp.sum(diff_lq1[i].astype(jnp.float32) * diff_lk1[i].astype(jnp.float32)))
               - jnp.exp(jnp.sum(diff_lq2[i].astype(jnp.float32) * diff_lk2[i].astype(jnp.float32)))
               + lam_init)

        shift, scale, gate = jnp.split(jax.nn.silu(c) @ w_ada[i] + b_ada[i], 3, axis=-1)
        shift_c, scale_c, gate_c = jnp.split(jax.nn.silu(c_ctx) @ w_ada[i] + b_ada[i], 3, axis=-1)
        h = rms_norm(x, norm_pre[i]) * (1.0 + scale[:, None]) + shift[:, None]
        hcn = rms_norm(hc, norm_pre[i]) * (1.0 + scale_c) + shift_c

        cq, ckv, kr, na_q, na_k, na_v, dq, dk, dv, g = jnp.split(h @ w_in[i], IN_SPLITS, axis=-1)
        ccq, cckv, ckr, cna_q, cna_k, cna_v, cdq, cdk, cdv, cg = jnp.split(hcn @ w_in[i], IN_SPLITS, axis=-1)

        m_kn_c, m_v_c = mla_keys(cckv, mla_kv_norm[i], w_ukv[i])
        na_kc, na_vc = split_heads(cna_k, NA_HEADS), split_heads(cna_v, NA_HEADS)
        d_kc = cdk.reshape(B, C, DIFF_HEADS, 2, DIFF_QK)
        d_vc = split_heads(cdv, DIFF_HEADS)

        m_qn, m_qr = mla_queries(cq, mla_q_norm[i], w_uq[i])
        m_qr = apply_axial_rope(m_qr, cos_h, sin_h)
        m_kn, m_v = mla_keys(ckv, mla_kv_norm[i], w_ukv[i])
        kn_all = jnp.concatenate([m_kn_c, m_kn], axis=1)
        kr_all = jnp.concatenate([ckr, apply_axial_rope(kr, cos, sin)], axis=1)
        v_all = jnp.concatenate([m_v_c, m_v], axis=1)
        o_mla = sweep_query_blocks(lambda qn, qr: mla_attend(qn, qr, kn_all, kr_all, v_all), m_qn, m_qr)

        o_na = na_latent(split_heads(na_q, NA_HEADS), split_heads(na_k, NA_HEADS),
                         split_heads(na_v, NA_HEADS), na_kc, na_vc, na_rpb[i])

        d_q = apply_axial_rope(dq.reshape(B, n, DIFF_HEADS, 2, DIFF_QK), cos_d, sin_d)
        d_k = apply_axial_rope(dk.reshape(B, n, DIFF_HEADS, 2, DIFF_QK), cos_d, sin_d)
        k1_all = jnp.concatenate([d_kc[..., 0, :], d_k[..., 0, :]], axis=1)
        k2_all = jnp.concatenate([d_kc[..., 1, :], d_k[..., 1, :]], axis=1)
        dv_all = jnp.concatenate([d_vc, split_heads(dv, DIFF_HEADS)], axis=1)
        o_diff = sweep_query_blocks(lambda q1, q2: diff_attend(q1, q2, k1_all, k2_all, dv_all, lam),
                                    d_q[..., 0, :], d_q[..., 1, :])
        o_diff = diff_post(o_diff, diff_subln[i], lam_init)

        y = mix_out(o_mla, o_na, o_diff, g, w_out[i])
        new_x = x + gate[:, None] * rms_norm(y, norm_post[i])

        if not last:
            cm_qn, cm_qr = mla_queries(ccq, mla_q_norm[i], w_uq[i])
            oc_mla = mla_attend(cm_qn, cm_qr, m_kn_c, ckr, m_v_c)
            oc_na = dense_attend(split_heads(cna_q, NA_HEADS), na_kc, na_vc)
            cd_q = cdq.reshape(B, C, DIFF_HEADS, 2, DIFF_QK)
            oc_diff = diff_post(diff_attend(cd_q[..., 0, :], cd_q[..., 1, :], d_kc[..., 0, :],
                                            d_kc[..., 1, :], d_vc, lam), diff_subln[i], lam_init)
            yc = mix_out(oc_mla, oc_na, oc_diff, cg, w_out[i])
            hc = hc + gate_c * rms_norm(yc, norm_post[i])
        x = new_x
    return x


_drawn_inputs = setup_inputs


def setup_inputs(seed=0):
    import zlib

    import numpy as np

    out = dict(_drawn_inputs(seed))
    spreads = {}
    factors = {'norm_pre': 4.555,
     'norm_post': 6.424,
     'mla_q_norm': 8.0,
     'mla_kv_norm': 8.0,
     'na_rpb': 8.0,
     'diff_subln': 7.524}
    for name, (base, spread) in spreads.items():
        noise = np.random.default_rng([zlib.crc32(name.encode()), seed]).standard_normal(out[name].shape)
        drawn = base * np.exp(spread * noise) if base else spread * noise
        out[name] = __import__('jax').numpy.asarray(drawn.astype(out[name].dtype))
    for name, factor in factors.items():
        out[name] = (out[name] * factor).astype(out[name].dtype)
    return out
```

```python
import math
from contextlib import ExitStack

import numpy as np
import concourse.bass as bass
from concourse import mybir

F32 = mybir.dt.float32
F32R = mybir.dt.float32r
ALU = mybir.AluOpType
ACT = mybir.ActivationFunctionType
AX = mybir.AxisListType

P = 128
D = 2048
KT = D // P
CTX = 256
SEQ = 256
TOK = CTX + SEQ
LAT = slice(CTX, TOK)
LAYERS = 2
GRID_W = 64
ROT = 64
THETA = 10000.0
EPS = 1e-6
MLA_H, NA_H, DIFF_H = 6, 5, 5
HEADS = MLA_H + NA_H + DIFF_H
NOPE, ROPE = 128, 64
Q_RANK, KV_RANK = 512, 256
RPB_R, RPB_C = 15, 31
WIN_W = 16
NEG = -1.0e30

C_CQ = 0
C_CKV = Q_RANK
C_KR = C_CKV + KV_RANK
C_NA = C_KR + ROPE
C_DIFF = C_NA + 3 * NA_H * P
C_G = C_DIFF + 3 * DIFF_H * P
IN_W = C_G + HEADS * P

T_ID, T_REV, T_ROT, T_ONE = 0, 128, 256, 384
T_COS, T_SIN, T_MASK, T_SEL = 512, 768, 1024, 1088
T_W = 1090

V_C, V_PRE, V_POST, V_QN, V_KVN, V_SUB, V_N = 0, 32, 64, 96, 104, 108, 110

ADA_UNITS = 3 * D // 512
PRE_TILES = 7
LAYER_TILES = PRE_TILES + 2 * MLA_H + 4 * NA_H + 4 * DIFF_H + KT
HEAD_TILES = 4


def tables():
    t = np.zeros((P, T_W), np.float32)
    t[:, T_ID:T_ID + P] = np.eye(P, dtype=np.float32)
    for p in range(P):
        t[p, T_REV + 64 * (p // 64) + 63 - p % 64] = 1.0
    q = ROT // 4
    for b in range(2):
        for i in range(ROT):
            src, sign = (i + q, -1.0) if (i // q) % 2 == 0 else (i - q, 1.0)
            t[64 * b + src, T_ROT + 64 * b + i] = sign
    t[:, T_ONE:T_ONE + P] = 1.0
    n = np.arange(SEQ)
    half = ROT // 2
    inv = (1.0 / (np.float32(THETA) ** (np.arange(0, half, 2, dtype=np.float32) / np.float32(half)))).astype(np.float32)
    ar = (n // GRID_W).astype(np.float32)[:, None] * inv[None]
    ac = (n % GRID_W).astype(np.float32)[:, None] * inv[None]
    ang = np.concatenate([ar, ar, ac, ac], axis=-1).astype(np.float32).T
    t[:, T_COS:T_COS + SEQ] = np.tile(np.cos(ang), (2, 1))
    t[:, T_SIN:T_SIN + SEQ] = np.tile(np.sin(ang), (2, 1))
    for p in range(P):
        qc = 63 - p % 64
        lo = min(max(qc - WIN_W // 2, 0), GRID_W - WIN_W)
        t[p, T_MASK:T_MASK + GRID_W] = NEG
        t[p, T_MASK + lo:T_MASK + lo + WIN_W] = 0.0
    t[0:2, T_SEL] = 1.0
    t[2:4, T_SEL + 1] = 1.0
    t[4, T_SEL:T_SEL + 2] = 1.0
    return t


class Tile:

    def __init__(self, first, i=0, per=4):
        self.n = first + per * i
        self.raw = first % 4
        self.split = first % 2
        self.round = first // 4 + (per // 4) * i
        self.first, self.i, self.per = first, i, per

    def ahead(self, k):
        return Tile(self.first + k, self.i, self.per)


class Banks:

    def __init__(self, phases):
        self.plan = {}
        fills, uses = [0] * 8, [0] * 8
        for key, trips, groups in phases:
            step_f, step_u = [0] * 8, [0] * 8
            at = {}
            for name, b, by_tile in groups:
                at[name] = (b, step_u[b], step_f[b])
                step_u[b] += 1
                step_f[b] += not by_tile
            self.plan[key] = (list(uses), list(fills), step_u, step_f, at)
            for b in range(8):
                uses[b] += trips * step_u[b]
                fills[b] += trips * step_f[b]

    def bank(self, key, name):
        return self.plan[key][4][name][0]

    def before(self, key, name, i=0):
        uses, _, step, _, at = self.plan[key]
        b, u, _ = at[name]
        return uses[b] + u + step[b] * i

    def filled(self, key, name, i=0):
        _, fills, _, step, at = self.plan[key]
        b, _, f = at[name]
        return fills[b] + f + 1 + step[b] * i


def head_groups(kind, L, j=0):
    s = str(j)
    if kind == "mla":
        a, b = (0, 1) if j == 0 else (1, 0)
        g = [("qn" + s, a, False), ("qr" + s, b, False), ("kn" + s, a, False), ("v" + s, b, True),
             ("g" + s, a, True), ("rot" + s, 7, False)]
    else:
        g = [("q" + s, 0, True), ("k" + s, 1, True), ("v" + s, 0, True), ("g" + s, 1, True)]
        if kind == "diff":
            g += [("rot" + s, 7, False)]
    g += [("vn" + s, 5, False)]
    for name, b in score_banks(kind, L):
        g += [(name + s, b, False)]
    g += [("pt_lat0" + s, 6, False), ("pt_lat1" + s, 5, False)]
    if L == 0:
        g += [("pt_ctx" + s, 6, False)]
    g += [("o" + s, 7, False)]
    if kind == "diff":
        g += [("ss" + s, 6, False)]
    return g


def score_banks(kind, L):
    if kind == "diff":
        s = [("s_lat0a", 2), ("s_lat0b", 3), ("s_lat1a", 4), ("s_lat1b", 2)]
        return s + ([("s_ctxa", 3), ("s_ctxb", 4)] if L == 0 else [])
    s = [("s_lat0", 2), ("s_lat1", 3)]
    return s + ([("s_ctx", 4)] if L == 0 else [])


def psum_plan():
    ph = [("vec", 1, [("vt", 0, False)])]
    ph += [("x", 1, [(f"x{d}", (d + 1) % 8, False) for d in range(KT)])]
    ph += [("sumx", 1, [("ssx0", 2, True)])]
    for L in range(LAYERS):
        ph += [(("ada", L), ADA_UNITS // 2, [("row0", 0, True), ("col0", 2, False), ("row1", 1, True), ("col1", 3, False)])]
    for L in range(LAYERS):
        ph += [(("pre", L), 1, [("ssx0", 2, True), ("ssx1", 3, True)][:2 * L] + [(f"t{t}", t % 2, True) for t in range(PRE_TILES)]
                + [("ssq", 2, True), ("sskv", 3, True), ("rot", 7, False)])]
        ph += [(("mla", L), MLA_H // 2, head_groups("mla", L, 0) + head_groups("mla", L, 1))]
        ph += [(("na", L), NA_H, head_groups("na", L))]
        ph += [(("diff", L), DIFF_H, head_groups("diff", L))]
        ph += [(("out", L), KT // 4, [(f"y{t}", t % 2, True) for t in range(4)])]
        ph += [(("post", L), 1, [("ssy", 4, False)])]
    ph += [("final", 1, [(f"o{g}", g, False) for g in range(8)])]
    return Banks(ph)


def backbone(nc, table, x, c, ctx_in, c_ctx, w_ada, b_ada, norm_pre, norm_post, w_in, mla_q_norm, mla_kv_norm,
             w_uq, w_ukv, na_rpb, diff_lq1, diff_lk1, diff_lq2, diff_lk2, diff_subln, w_out, out):
    banks = psum_plan()
    stack = ExitStack()
    with stack:
        sem_names = []

        def sem(name):
            sem_names.append(name)
            return stack.enter_context(nc.semaphore(name))

        base = (nc.sbuf_base + 63) // 64 * 64
        KB = 1024

        def at(name, shape, off, dt=F32):
            return nc.alloc_sbuf_tensor_at(name, shape, dt, offset=base + off)

        Z = at("residual_mixed_out", [P, KT, TOK], 0)
        hh = at("act_hi", [P, KT, TOK], 32 * KB, F32R)
        hl = at("act_lo", [P, KT, TOK], 64 * KB, F32R)
        xin = at("tokens_in", [P, 4, D], 64 * KB)
        oout = at("tokens_out", [P, 2, D], 64 * KB)
        raw = at("w_raw", [P, 4, 2048], 96 * KB)
        wh = at("w_hi", [P, 2, 2048], 128 * KB, F32R)
        wl = at("w_lo", [P, 2, 2048], 144 * KB, F32R)
        cqh = at("cq_hi", [P, 4, TOK], 12 * KB, F32R)
        cql = at("cq_lo", [P, 4, TOK], 20 * KB, F32R)
        kvh = at("ckv_hi", [P, 2, TOK], 28 * KB, F32R)
        off = 160 * KB
        tab = at("tables", [P, T_W], off)
        off += T_W * 4 + 24
        qk = at("qk", [P, 2, TOK], off)
        off += 4 * KB
        vT = at("vT", [P, TOK], off)
        off += 2 * KB
        vN = at("vN", [P, 4, P], off)
        off += 2 * KB
        qr = at("q_rot", [P, TOK], off)
        kr = at("k_rot", [P, TOK], off + 2 * KB)
        xback = at("residual_back", [P, KT, SEQ], off - 8 * KB)
        bt = at("bias_raw", [P, 6 * GRID_W], off)
        btm = at("bias_masked", [P, 6 * GRID_W], off + 2 * KB)
        off += 4 * KB
        probs = at("probs", [P, 2, 3, TOK], off)
        kvraw = at("ckv_raw", [P, 2, TOK], off)
        cqraw = at("cq_raw", [P, 4, TOK], off + 4 * KB)
        kvl = at("ckv_lo", [P, 2, TOK], off + 8 * KB, F32R)
        arow = at("ada_rows", [5, 2, 512], off)
        vrows = at("vec_rows", [V_N, P], off + 4 * KB)
        off += 12 * KB
        ptl = at("probsT_lat", [P, 4, SEQ], off)
        sqx = at("squares", [P, 3, TOK], off)
        ptc = at("probsT_ctx", [P, 2, CTX], off + 4 * KB)
        off += 6 * KB
        tmp = at("tmp", [P, 4, TOK], off)
        lamr = at("lam_rows", [P, LAYERS * 4, DIFF_QK_], off)
        off += 8 * KB
        rs = at("rstd", [P, TOK], off)
        off += 2 * KB
        vcol = at("vec_cols", [P, V_N], off)
        off += 448
        ada = at("ada_cols", [P, LAYERS, 48, 2], off)
        off += 768
        A = at("scale_cols", [P, LAYERS, KT, 2], off)
        off += 256
        G = at("gate_cols", [P, LAYERS, KT, 2], off)
        off += 256
        cst = at("c_split", [P, 4 * KT + P], off, F32R)
        off += 768
        stat = at("stats", [P, 48], off)
        off += 192
        assert base + off <= nc.sbuf_usable_end
        nmx = stat[:, 0:12].rearrange("p (m r q) -> p m r q", m=2, r=3)
        sm = stat[:, 12:24].rearrange("p (m r q) -> p m r q", m=2, r=3)
        rc = stat[:, 24:36].rearrange("p (m r q) -> p m r q", m=2, r=3)
        neglam = stat[:, 36:38]
        ldot = stat[:, 38:42].rearrange("p (l t) -> p l t", l=2)
        lexp = stat[:, 42:46].rearrange("p (l t) -> p l t", l=2)
        subc = stat[:, 46:48]
        sq = [tmp[:, 0, :], tmp[:, 1, :]]
        acc = tmp[:, 2, :]
        gs, ge = tmp[:, 2, :], tmp[:, 3, :]

        ident = tab[:, T_ID:T_ID + P]
        rev = tab[:, T_REV:T_REV + P]
        rotm = tab[:, T_ROT:T_ROT + P]
        ones = tab[:, T_ONE:T_ONE + P]
        cos = tab[:, T_COS:T_COS + SEQ]
        sin = tab[:, T_SIN:T_SIN + SEQ]
        mask = tab[:, T_MASK:T_MASK + GRID_W]
        sel = tab[0:5, T_SEL:T_SEL + 2]

        ps = [stack.enter_context(nc.psum_tensor(f"bank{b}", [P, 512], F32)) for b in range(8)]
        spill = nc.dram_tensor("residual_spill", [P, KT, TOK], F32, kind="Internal").ap()

        filled = [sem(f"bank_filled{b}") for b in range(8)]
        emptied = [sem(f"bank_emptied{b}") for b in range(8)]
        raw_loaded = [sem(f"raw_loaded{b}") for b in range(4)]
        ukv_loaded = sem("ukv_loaded")
        hi_done = sem("hi_done")
        lo_done = sem("lo_done")
        tile_used = sem("tile_used")
        tab_loaded = sem("tab_loaded")
        vec_loaded = sem("vec_loaded")
        x_loaded = sem("x_loaded")
        lam_loaded = sem("lam_loaded")
        brow_loaded = [sem(f"brow_loaded{j}") for j in range(2)]
        rpb_loaded = sem("rpb_loaded")
        c_exp = sem("c_exp")
        c_ready = sem("c_ready")
        lam_dot = sem("lam_dot")
        lam_exp = sem("lam_exp")
        consts_ready = sem("consts_ready")
        xsq_ready = sem("xsq_ready")
        ysq_ready = sem("ysq_ready")
        acc_ready = sem("acc_ready")
        ms_ready = sem("ms_ready")
        root_ready = sem("root_ready")
        rstd_ready = sem("rstd_ready")
        hval = sem("hval")
        sq_used = sem("sq_used")
        ylo = sem("ylo")
        hhi = sem("hhi")
        yhi = sem("yhi")
        chi = sem("chi")
        hlo = sem("hlo")
        clo = sem("clo")
        cnorm = sem("cnorm")
        roped = sem("roped")
        max_done = [sem(f"max_done_{r}") for r in ("lat0", "lat1", "ctx")]
        norm_done = [sem(f"norm_done_{r}") for r in ("lat0", "lat1", "ctx")]
        dsq_ready = sem("dsq_ready")
        dms_ready = sem("dms_ready")
        droot_ready = sem("droot_ready")
        bias_built = sem("bias_built")
        spilled = sem("spilled")
        back = sem("back")
        xnew = sem("xnew")
        dve_chain = sem("dve_chain")
        o_ready = sem("o_ready")
        stored = sem("stored")

        ada0 = [L * ADA_UNITS * 4 for L in range(LAYERS)]
        first = [LAYERS * ADA_UNITS * 4 + L * LAYER_TILES for L in range(LAYERS)]
        mla0 = [f + PRE_TILES for f in first]
        na0 = [f + 2 * MLA_H for f in mla0]
        diff0 = [f + 4 * NA_H for f in na0]
        out0 = [f + 4 * DIFF_H for f in diff0]
        last_tile = out0[-1] + KT - 1
        ropes = 1 + MLA_H + DIFF_H
        half = [slice(0, CTX), LAT]
        stream = [1, 0]

        def qcols(L):
            return slice(0, TOK) if L == 0 else LAT

        def act_halves(L):
            return (1, 0) if L == 0 else (1,)

        def mod_groups(L):
            return [(slice(0, TOK), (0, 1))] if L == 0 else [(LAT, (1,)), (slice(0, CTX), (0,))]

        mod0 = [0, KT]

        def row_groups(L):
            return (0, 1, 2) if L == 0 else (0, 1)

        def score_names(kind, L, r):
            nm = ("s_lat0", "s_lat1", "s_ctx")[r]
            return [nm + "a", nm + "b"] if kind == "diff" else [nm]

        block = stack.enter_context(nc.Block())

        @block.sync
        def _(sp):
            def load(t, src, dst):
                if not isinstance(t.n, int) or t.n >= 4:
                    sp.wait_ge(lo_done, t.n - 3)
                sp.dma_start(dst, src).then_inc(raw_loaded[t.raw], 16)

            def slot(t, c):
                return raw[:, t.raw, :].rearrange("p (k c) -> p k c", c=c)

            def w_cols(w, L, col):
                return w[L].rearrange("(k p) n -> p k n", p=P)[:, :, col]

            sp.dma_start(tab[:, :], table).then_inc(tab_loaded, 16)
            rows = [(V_C, c.rearrange("a (r p) -> (a r) p", p=P)), (V_C + 16, c_ctx.rearrange("(r p) -> r p", p=P)),
                    (V_PRE, norm_pre.rearrange("l (r p) -> (l r) p", p=P)),
                    (V_POST, norm_post.rearrange("l (r p) -> (l r) p", p=P)),
                    (V_QN, mla_q_norm.rearrange("l (r p) -> (l r) p", p=P)),
                    (V_KVN, mla_kv_norm.rearrange("l (r p) -> (l r) p", p=P)), (V_SUB, diff_subln)]
            for r0, src in rows:
                sp.dma_start(vrows[r0:r0 + src.shape[0], :], src).then_inc(vec_loaded, 16)
            for t in range(4):
                load(Tile(t), ada_src(w_ada, 0, t, 0), slot(Tile(t), 512))
            sp.dma_start(xin[:, 0:2, :], ctx_in[0].rearrange("(b p) d -> p b d", p=P)).then_inc(x_loaded, 16)
            sp.dma_start(xin[:, 2:4, :], x[0].rearrange("(b p) d -> p b d", p=P)).then_inc(x_loaded, 16)
            for L in range(LAYERS):
                for k, v in enumerate((diff_lq1, diff_lk1, diff_lq2, diff_lk2)):
                    src = bass.AP(v.tensor, L * DIFF_QK_, [[0, P], [1, DIFF_QK_]])
                    sp.dma_start(lamr[:, 4 * L + k, :], src).then_inc(lam_loaded, 16)

            def ada_brow(L, i, j):
                if L or not isinstance(i, int):
                    sp.wait_ge(filled[2 + j], banks.filled(("ada", L), f"col{j}", i) - 1)
                sp.dma_start(arow[4:5, j, :], b_ada[L:L + 1, bass.ds(512 * (2 * i + j), 512)]).then_inc(brow_loaded[j], 16)

            for L in range(LAYERS):
                def ada_unit(i, j):
                    ada_brow(L, i, j)
                    for t in range(4):
                        tl = Tile(ada0[L] + 4 * j + t, i, 8)
                        load(tl, ada_src(w_ada, L, t, 512 * (2 * i + j)), slot(tl, 512))

                if L == 0:
                    ada_brow(0, 0, 0)
                    ada_brow(0, 0, 1)
                    for t in range(4):
                        tl = Tile(4 + t)
                        load(tl, ada_src(w_ada, 0, t, 512), slot(tl, 512))
                    with sp.Fori(1, ADA_UNITS // 2) as i:
                        ada_unit(i, 0)
                        ada_unit(i, 1)
                else:
                    with sp.Fori(0, ADA_UNITS // 2) as i:
                        ada_unit(i, 0)
                        ada_unit(i, 1)

            for L in range(LAYERS):
                for t in range(PRE_TILES):
                    tl = Tile(first[L] + t)
                    load(tl, w_cols(w_in, L, slice(P * t, P * t + P)), slot(tl, P))
                with sp.Fori(0, MLA_H // 2) as i:
                    for j in range(2):
                        tl = Tile(mla0[L] + 2 * j, i)
                        sp.wait_ge(lo_done, tl.n - 3)
                        uq = w_uq[L].rearrange("(k p) n -> p k n", p=P)[:, :, bass.ds((2 * i + j) * (NOPE + ROPE), NOPE + ROPE)]
                        ukv = w_ukv[L].rearrange("(k p) n -> p k n", p=P)[:, :, bass.ds((2 * i + j) * 256, 256)]
                        sp.dma_start(raw[:, tl.raw, 768:1280].rearrange("p (k c) -> p k c", c=256), ukv).then_inc(ukv_loaded, 16)
                        sp.wait_ge(ukv_loaded, 16 * (L * MLA_H + j + 1) + 32 * i)
                        sp.dma_start(raw[:, tl.raw, 0:768].rearrange("p (k c) -> p k c", c=192), uq).then_inc(raw_loaded[tl.raw], 16)
                        tg = tl.ahead(1)
                        load(tg, w_cols(w_in, L, bass.ds(C_G + P * (2 * i + j), P)), slot(tg, P))
                with sp.Fori(0, NA_H) as i:
                    tl = Tile(na0[L], i)
                    for k, col in enumerate((C_NA, C_NA + NA_H * P, C_NA + 2 * NA_H * P, C_G + MLA_H * P)):
                        load(tl.ahead(k), w_cols(w_in, L, bass.ds(col + P * i, P)), slot(tl.ahead(k), P))
                    sp.wait_ge(tile_used, tl.n + 1)
                    for s in range(2):
                        src = bass.AP(na_rpb.tensor, L * NA_H * RPB_R * RPB_C + (5 - s) * RPB_C - 48 + i * (RPB_R * RPB_C),
                                      [[1, 64], [RPB_C, 6], [1, GRID_W]])
                        dst = bt[64 * s:64 * s + 64, :].rearrange("p (r c) -> p r c", c=GRID_W)
                        sp.dma_start(dst, src).then_inc(rpb_loaded, 16)
                with sp.Fori(0, DIFF_H) as i:
                    tl = Tile(diff0[L], i)
                    for k, col in enumerate((C_DIFF, C_DIFF + DIFF_H * P, C_DIFF + 2 * DIFF_H * P, C_G + (MLA_H + NA_H) * P)):
                        load(tl.ahead(k), w_cols(w_in, L, bass.ds(col + P * i, P)), slot(tl.ahead(k), P))
                with sp.Fori(0, KT // 4) as i:
                    for k in range(4):
                        tl = Tile(out0[L] + k, i)
                        load(tl, w_cols(w_out, L, bass.ds(4 * P * i + P * k, P)), slot(tl, P))
            for g in range(8):
                q, blk = g // 2, g % 2
                sp.wait_ge(o_ready, g + 1)
                sp.dma_start(out[0, P * blk:P * blk + P, 512 * q:512 * q + 512],
                             oout[:, blk, 512 * q:512 * q + 512]).then_inc(stored, 16)
            sp.wait_ge(stored, 16 * 8)

        @block.gpsimd
        def _(pool):
            pool.wait_ge(tab_loaded, 16)
            m = 0
            for L in range(LAYERS):
                for cols, _ in mod_groups(L):
                    for t in range(KT):
                        pool.wait_ge(hhi, m + 1)
                        nc.gpsimd.tensor_tensor(hl[:, t, cols], tmp[:, m % 4, cols], hh[:, t, cols].bitcast(F32),
                                                ALU.subtract).then_inc(hlo, 1)
                        m += 1
                with pool.Fori(0, NA_H) as i:
                    pool.wait_ge(rpb_loaded, 32 * (L * NA_H + 1) + 32 * i)
                    nc.gpsimd.tensor_tensor(btm[:, :].rearrange("p (r c) -> p r c", c=GRID_W),
                                            bt[:, :].rearrange("p (r c) -> p r c", c=GRID_W),
                                            mask[:, None, :].to_broadcast([P, 6, GRID_W]), ALU.add).then_inc(bias_built, 1)

        @block.scalar
        def _(act):
            def bank_of(key, name):
                b = banks.bank(key, name)
                return b, ps[b]

            def wait_filled(key, name, i=0):
                b = banks.bank(key, name)
                act.wait_ge(filled[b], banks.filled(key, name, i))
                return b

            def split_hi(t):
                act.wait_ge(raw_loaded[t.raw], 16 * (t.round + 1))
                if not isinstance(t.n, int) or t.n >= 2:
                    act.wait_ge(tile_used, t.n - 1)
                nc.scalar.activation(wh[:, t.split, :], raw[:, t.raw, :], ACT.Copy).then_inc(hi_done, 1)

            act.wait_ge(filled[0], banks.filled("vec", "vt"))
            nc.scalar.activation(tmp[:, 3, 0:32], ps[0][:, 0:32], ACT.Exp, scale=-1.0).then_inc(c_exp, 1)
            act.wait_ge(lam_dot, LAYERS)
            nc.scalar.activation(lexp, ldot, ACT.Exp).then_inc(lam_exp, 1)
            items = dict(xsq=0, ysq=0, root=0, mod=0, ylo=0, c=0, back=0, xnew=0)

            def squares(src, cols):
                k = items["xsq"]
                if k >= 3:
                    act.wait_ge(sq_used, k - 2)
                nc.scalar.activation(sqx[:, k % 3, cols], src, ACT.Square).then_inc(xsq_ready, 1)
                items["xsq"] = k + 1

            def take_root(cols):
                items["root"] += 1
                act.wait_ge(ms_ready, items["root"])
                nc.scalar.activation(rs[:, cols], rs[:, cols], ACT.Sqrt).then_inc(root_ready, 1)

            def modulated_hi(cols):
                for t in range(KT):
                    m = items["mod"]
                    act.wait_ge(hval, m + 1)
                    nc.scalar.activation(hh[:, t, cols], tmp[:, m % 4, cols], ACT.Copy).then_inc(hhi, 1)
                    items["mod"] = m + 1

            def new_squares(cols):
                for t in range(KT):
                    items["xnew"] += 1
                    act.wait_ge(xnew, items["xnew"])
                    squares(Z[:, t, cols], cols)

            for d in range(KT):
                b = wait_filled("x", f"x{d}")
                nc.scalar.activation(Z[:, d, :], ps[b][:, :], ACT.Copy).then_inc(emptied[b], 1)
            for d in range(KT):
                b = banks.bank("x", f"x{d}")
                act.wait_ge(emptied[b], banks.before("x", f"x{d}") + 1)
                squares(Z[:, d, :], slice(0, TOK))
            act.dma_start(spill, Z[:, :, :]).then_inc(spilled, 16)
            take_root(slice(0, TOK))

            split_hi(Tile(0))
            split_hi(Tile(1))
            for L in range(LAYERS):
                with act.Fori(0, ADA_UNITS // 2) as i:
                    for j in range(2):
                        for t in range(4):
                            tl = Tile(ada0[L] + 4 * j + t, i, 8)
                            if t == 3:
                                act.wait_ge(tile_used, tl.n + 1)
                                b, bank = bank_of(("ada", L), f"row{j}")
                                nc.scalar.activation(arow[0:4, j, :], bank[0:4, :], ACT.Copy).then_inc(emptied[b], 1)
                            split_hi(tl.ahead(2))

            def head(kind, L, i, j, tq, tg, H, D_no):
                key, s = (kind, L), str(j)
                Q = qcols(L)
                scale = {"mla": (NOPE + ROPE) ** -0.5, "na": P ** -0.5, "diff": ROT ** -0.5}[kind]
                def exps(r):
                    act.wait_ge(max_done[r], H + 1)
                    for m, name in enumerate(score_names(kind, L, r)):
                        b, bank = bank_of(key, name + s)
                        if r < 2:
                            nc.scalar.activation(probs[:, m, r, :], bank[:, :], ACT.Exp, bias=nmx[:, m, r, 0:1],
                                                 accum_out=sm[:, m, r, 0:1]).then_inc(emptied[b], 1)
                        else:
                            for t in range(2):
                                e = nc.scalar.activation(probs[:, m, r, 256 * t:256 * t + 256], bank[:, 256 * t:256 * t + 256],
                                                         ACT.Exp, bias=nmx[:, m, r, t:t + 1], accum_out=sm[:, m, r, t:t + 1])
                            e.then_inc(emptied[b], 1)

                if kind == "mla":
                    b = wait_filled(key, "qn" + s, i)
                    nc.scalar.activation(qk[:, 0, Q], ps[b][:, Q], ACT.Copy, scale=scale).then_inc(emptied[b], 1)
                    b = wait_filled(key, "qr" + s, i)
                    nc.scalar.activation(qr[0:64, Q], ps[b][0:64, Q], ACT.Copy, scale=scale).then_inc(emptied[b], 1)
                    b = wait_filled(key, "kn" + s, i)
                    nc.scalar.activation(qk[:, 1, :], ps[b][:, :], ACT.Copy).then_inc(emptied[b], 1)
                    act.wait_ge(tile_used, tq.n + 1)
                    b, bank = bank_of(key, "v" + s)
                    nc.scalar.activation(vT[:, :], bank[:, :], ACT.Copy).then_inc(emptied[b], 1)
                    split_hi(tq.ahead(2))
                    for r in row_groups(L):
                        exps(r)
                else:
                    act.wait_ge(tile_used, tq.n + 1)
                    b, bank = bank_of(key, "q" + s)
                    nc.scalar.activation(qk[:, 0, Q], bank[:, Q], ACT.Copy, scale=scale).then_inc(emptied[b], 1)
                    split_hi(tq.ahead(2))
                    act.wait_ge(tile_used, tq.ahead(1).n + 1)
                    b, bank = bank_of(key, "k" + s)
                    nc.scalar.activation(qk[:, 1, :], bank[:, :], ACT.Copy).then_inc(emptied[b], 1)
                    split_hi(tq.ahead(3))
                    for r in row_groups(L):
                        exps(r)
                    act.wait_ge(tile_used, tq.ahead(2).n + 1)
                    b, bank = bank_of(key, "v" + s)
                    nc.scalar.activation(vT[:, :], bank[:, :], ACT.Copy).then_inc(emptied[b], 1)
                    split_hi(tq.ahead(4))
                for r in row_groups(L):
                    b = wait_filled(key, ("pt_lat0", "pt_lat1", "pt_ctx")[r] + s, i)
                    if r < 2:
                        dst, src = ptl[:, :, P * r:P * r + P], ps[b][:, :].rearrange("p (k q) -> p k q", q=P)
                    else:
                        dst, src = ptc[:, :, :], ps[b][:, :].rearrange("p (k q) -> p k q", q=CTX)
                    nc.scalar.activation(dst, src, ACT.Copy).then_inc(emptied[b], 1)
                if kind == "diff":
                    b = wait_filled(key, "o" + s, i)
                    nc.scalar.activation(sq[1][:, Q], ps[b][:, Q], ACT.Square).then_inc(dsq_ready, 1)
                    act.wait_ge(dms_ready, D_no + 1)
                    nc.scalar.activation(rs[:, Q], rs[:, Q], ACT.Sqrt).then_inc(droot_ready, 1)
                split_hi(tg.ahead(2))
                b7 = "rot" + s if kind != "na" else "o" + s
                act.wait_ge(emptied[7], banks.before(key, b7, i))
                b, bank = bank_of(key, "g" + s)
                nc.scalar.activation(gs[:, Q], bank[:, Q], ACT.Copy)
                nc.scalar.activation(ge[:, Q], bank[:, Q], ACT.Exp, scale=-1.0).then_inc(emptied[b], 1)

            act.wait_ge(consts_ready, 1)
            for L in range(LAYERS):
                key = ("pre", L)
                Q = qcols(L)

                def pre_tile(t):
                    tl = Tile(first[L] + t)
                    act.wait_ge(tile_used, tl.n + 1)
                    b, bank = bank_of(key, f"t{t}")
                    if t < 6:
                        cols = Q if t < 4 else slice(0, TOK)
                        dst = cqraw[:, t, cols] if t < 4 else kvraw[:, t - 4, cols]
                        squares(bank[:, cols], cols)
                        nc.scalar.activation(dst, bank[:, cols], ACT.Copy).then_inc(emptied[b], 1)
                    else:
                        nc.scalar.activation(kr[:, :], bank[:, :], ACT.Copy).then_inc(emptied[b], 1)
                    split_hi(tl.ahead(2))

                if L == 0:
                    modulated_hi(slice(0, TOK))
                    pre_tile(0)
                    pre_tile(1)
                else:
                    pre_tile(0)
                    take_root(slice(0, CTX))
                    new_squares(slice(0, CTX))
                    pre_tile(1)
                    take_root(slice(0, CTX))
                    modulated_hi(slice(0, CTX))
                for t in range(2, PRE_TILES):
                    pre_tile(t)
                act.wait_ge(spilled, 16 * (L + 1))
                for nt, dsth in ((4, cqh), (2, kvh)):
                    cols = Q if nt == 4 else slice(0, TOK)
                    take_root(cols)
                    for t in range(nt):
                        items["c"] += 1
                        act.wait_ge(cnorm, items["c"])
                        nc.scalar.activation(dsth[:, t, cols], tmp[:, t % 2, cols], ACT.Copy).then_inc(chi, 1)
                with act.Fori(0, MLA_H // 2) as i:
                    for j in range(2):
                        tq = Tile(mla0[L] + 2 * j, i)
                        head("mla", L, i, j, tq, tq.ahead(1), HEADS * L + j + 2 * i, None)
                with act.Fori(0, NA_H) as i:
                    tq = Tile(na0[L], i)
                    head("na", L, i, 0, tq, tq.ahead(3), HEADS * L + MLA_H + i, None)
                with act.Fori(0, DIFF_H) as i:
                    tq = Tile(diff0[L], i)
                    head("diff", L, i, 0, tq, tq.ahead(3), HEADS * L + MLA_H + NA_H + i, DIFF_H * L + i)
                act.wait_ge(filled[7], banks.filled(("diff", L), "o0", DIFF_H - 1))
                act.dma_start(xback[:, :, :], spill[:, :, LAT]).then_inc(back, 16)
                act.wait_ge(tile_used, out0[L])
                for t in range(KT):
                    if t == KT - 2:
                        act.wait_ge(emptied[7], banks.before(("diff", L), "o0", DIFF_H - 2) + 1)
                    if t == KT - 1:
                        act.wait_ge(emptied[7], banks.before(("diff", L), "o0", DIFF_H - 1) + 1)
                    nc.scalar.activation(hh[:, t, Q], Z[:, t, Q], ACT.Copy).then_inc(yhi, 1)

                def out_tile(i, k, ahead):
                    tl = Tile(out0[L] + k, i)
                    act.wait_ge(tile_used, tl.n + 1)
                    b, bank = bank_of(("out", L), f"y{k}")
                    if not (isinstance(i, int) and 4 * i + k < 2):
                        act.wait_ge(acc_ready, items["ysq"] + 4 * i + k - 1)
                    nc.scalar.activation(sq[k % 2][:, Q], bank[:, Q], ACT.Square).then_inc(ysq_ready, 1)
                    for a in act_halves(L):
                        g = G[:, L, bass.ds(4 * i + k, 1), stream[a]:stream[a] + 1].rearrange("p o s -> p (o s)")
                        last = nc.scalar.activation(Z[:, bass.ds(4 * i + k, 1), half[a]].rearrange("p o t -> p (o t)"),
                                                    bank[:, half[a]], ACT.Copy, scale=g)
                    last.then_inc(emptied[b], 1)
                    if ahead:
                        split_hi(tl.ahead(2))

                for k in range(4):
                    out_tile(0, k, True)
                with act.Fori(1, KT // 4 - 1) as i:
                    for k in range(4):
                        out_tile(i, k, True)
                for k in range(4):
                    out_tile(KT // 4 - 1, k, not (L == LAYERS - 1 and k >= 2))
                items["ysq"] += KT
                take_root(LAT)
                if L < LAYERS - 1:
                    new_squares(LAT)
                    act.dma_start(xback[:, :, :], spill[:, :, 0:CTX]).then_inc(back, 16)
                    act.wait_ge(back, 16 * (2 * L + 2))
                    act.dma_start(spill[:, :, LAT], Z[:, :, LAT]).then_inc(spilled, 16)
                    take_root(LAT)
                    modulated_hi(LAT)
            for g in range(8):
                q, blk = g // 2, g % 2
                b = wait_filled("final", f"o{g}")
                nc.scalar.activation(oout[:, blk, 512 * q:512 * q + 512], ps[b][:, :], ACT.Copy).then_inc(o_ready, 1)

        @block.vector
        def _(dve):
            links = [0]
            step = dict(i=0, per=0, k=0)

            def link(ins):
                step["k"] += 1
                ins.then_inc(dve_chain, 1)
                dve.wait_ge(dve_chain, links[0] + step["k"] + step["per"] * step["i"])

            def begin(i=0, per=0):
                step.update(i=i, per=per, k=0)

            def end(trips=1):
                if step["per"]:
                    assert step["k"] == step["per"], ("links of a step", step["k"])
                links[0] += step["k"] * trips

            def bank_of(key, name):
                b = banks.bank(key, name)
                return b, ps[b]

            def wait_filled(key, name, i=0):
                b = banks.bank(key, name)
                dve.wait_ge(filled[b], banks.filled(key, name, i))
                return b

            def wait_emptied(key, name, i=0):
                b = banks.bank(key, name)
                dve.wait_ge(emptied[b], banks.before(key, name, i) + 1)

            def split_lo(t):
                dve.wait_ge(hi_done, t.n + 1)
                nc.vector.tensor_tensor(wl[:, t.split, :], raw[:, t.raw, :], wh[:, t.split, :].bitcast(F32),
                                        ALU.subtract).then_inc(lo_done, 1)

            begin()
            link(nc.vector.memset(cst[:, :].bitcast(F32), 0.0))
            b = wait_filled("vec", "vt")
            dve.wait_ge(c_exp, 1)
            link(nc.vector.tensor_scalar(tmp[:, 3, 32:64], tmp[:, 3, 0:32], 1.0, None, ALU.add))
            link(nc.vector.reciprocal(tmp[:, 3, 64:96], tmp[:, 3, 32:64]))
            link(nc.vector.tensor_tensor(tmp[:, 3, 0:32], ps[b][:, 0:32], tmp[:, 3, 64:96], ALU.mult))
            nc.vector.tensor_copy(vcol[:, :], ps[b][:, 0:V_N]).then_inc(emptied[b], 1)
            csv = cst[:, 0:4 * KT].rearrange("p (k e) -> p k e", e=4)
            for s in range(2):
                link(nc.vector.tensor_copy(csv[:, :, 2 * s], tmp[:, 3, 16 * s:16 * s + 16]))
                last = nc.vector.tensor_tensor(csv[:, :, 2 * s + 1], tmp[:, 3, 16 * s:16 * s + 16],
                                               csv[:, :, 2 * s].bitcast(F32), ALU.subtract)
            last.then_inc(c_ready, 1)
            dve.wait_ge(lam_loaded, 16 * 4 * LAYERS)
            for L in range(LAYERS):
                for t in range(2):
                    last = nc.vector.tensor_tensor_reduce(lamr[:, 4 * L + 2 * t, :], lamr[:, 4 * L + 2 * t, :], lamr[:, 4 * L + 2 * t + 1, :],
                                                          1.0, 0.0, ALU.mult, ALU.add, ldot[:, L, t:t + 1])
                last.then_inc(lam_dot, 1)
            dve.wait_ge(lam_exp, 1)
            for L in range(LAYERS):
                lam_init = 0.8 - 0.6 * math.exp(-0.3 * L)
                link(nc.vector.tensor_tensor(neglam[:, L:L + 1], lexp[:, L, 1:2], lexp[:, L, 0:1], ALU.subtract))
                link(nc.vector.tensor_scalar(neglam[:, L:L + 1], neglam[:, L:L + 1], -lam_init, None, ALU.add))
            end()

            n = dict(root=0, mod=0, c=0, ysq=0, xsq=KT)

            def rstd(src, width, cols, emptied_bank=None, uses=0):
                nc.vector.tensor_scalar(rs[:, cols], src, 1.0 / width, EPS, ALU.mult, ALU.add).then_inc(ms_ready, 1)
                n["root"] += 1
                dve.wait_ge(root_ready, n["root"])
                if emptied_bank is None:
                    link(nc.vector.reciprocal(rs[:, cols], rs[:, cols]))
                else:
                    nc.vector.reciprocal(rs[:, cols], rs[:, cols]).then_inc(emptied[emptied_bank], 1)
                    dve.wait_ge(emptied[emptied_bank], uses)

            def rstd_of(key, name, width, cols):
                b = banks.bank(key, name)
                rstd(ps[b][:, cols], width, cols, b, banks.before(key, name) + 1)

            begin()
            dve.wait_ge(sq_used, KT)
            rstd_of("sumx", "ssx0", D, slice(0, TOK))
            end()

            split_lo(Tile(0))
            split_lo(Tile(1))
            for L in range(LAYERS):
                with dve.Fori(0, ADA_UNITS // 2) as i:
                    for j in range(2):
                        for t in range(4):
                            split_lo(Tile(ada0[L] + 4 * j + t, i, 8).ahead(2))
                        b = wait_filled(("ada", L), f"col{j}", i)
                        nc.vector.tensor_copy(ada[:, L, bass.ds(8 * i + 4 * j, 4), :],
                                              ps[b][:, 0:8].rearrange("p (u s) -> p u s", s=2)).then_inc(emptied[b], 1)
            for b in (2, 3):
                dve.wait_ge(emptied[b], banks.before(("ada", 1), f"col{b - 2}", ADA_UNITS // 2 - 1) + 1)
            begin()
            dve.wait_ge(emptied[0], 1)
            for L in range(LAYERS):
                pre = vcol[:, V_PRE + KT * L:V_PRE + KT * L + KT]
                post = vcol[:, V_POST + KT * L:V_POST + KT * L + KT]
                for s in range(2):
                    nc.vector.scalar_tensor_tensor(out=A[:, L, :, s], in0=ada[:, L, 16:32, s], scalar=1.0, in1=pre,
                                                   op0=ALU.add, op1=ALU.mult)
                    nc.vector.tensor_tensor(G[:, L, :, s], ada[:, L, 32:48, s], post, ALU.mult)
                lam_init = 0.8 - 0.6 * math.exp(-0.3 * L)
                last = nc.vector.tensor_scalar(subc[:, L:L + 1], vcol[:, V_SUB + L:V_SUB + L + 1], 1.0 - lam_init, None, ALU.mult)
            last.then_inc(consts_ready, 1)
            dve.wait_ge(consts_ready, 1)
            end()

            def modulate(L, cols, halves):
                for t in range(KT):
                    m = n["mod"]
                    v = tmp[:, m % 4, :]
                    if m >= 4:
                        dve.wait_ge(hlo, m - 3)
                    link(nc.vector.tensor_tensor(v[:, cols], Z[:, t, cols], rs[:, cols], ALU.mult))
                    for a in halves:
                        e = stream[a]
                        last = nc.vector.tensor_scalar(v[:, half[a]], v[:, half[a]], A[:, L, t, e:e + 1], ada[:, L, t, e:e + 1],
                                                       ALU.mult, ALU.add)
                    last.then_inc(hval, 1)
                    n["mod"] = m + 1

            def new_residual(cols, part):
                dve.wait_ge(back, 16 * part)
                for t in range(KT):
                    link(nc.vector.tensor_tensor(Z[:, t, cols], Z[:, t, cols], rs[:, cols], ALU.mult))
                    nc.vector.tensor_tensor(Z[:, t, cols], Z[:, t, cols], xback[:, t, :], ALU.add).then_inc(xnew, 1)

            def rope(key, name, i, bufs, rows):
                b = wait_filled(key, name, i)
                nb = bufs.shape[1]
                src = ps[b][rows, 0:256 * nb].rearrange("p (a t) -> p a t", a=nb)
                t = tmp[rows, 0, 0:256 * nb].rearrange("p (a t) -> p a t", a=nb)
                cs, sn = (v[rows, None, :].to_broadcast([src.shape[0], nb, SEQ]) for v in (cos, sin))
                nc.vector.tensor_tensor(t, src, sn, ALU.mult).then_inc(emptied[b], 1)
                link(nc.vector.tensor_tensor(bufs, bufs, cs, ALU.mult))
                dve.wait_ge(emptied[b], banks.before(key, name, i) + 1)
                nc.vector.tensor_tensor(bufs, bufs, t, ALU.add).then_inc(roped, 1)

            def head(kind, L, i, j, tq, tg, H, y_at, D_no):
                key, s = (kind, L), str(j)
                Q = qcols(L)
                def values():
                    b = wait_filled(key, "vn" + s, i)
                    nc.vector.tensor_copy(vN[:, :, :], ps[b][:, :].rearrange("p (k d) -> p k d", d=P)).then_inc(emptied[b], 1)

                def maxima(r):
                    for m, name in enumerate(score_names(kind, L, r)):
                        b = wait_filled(key, name + s, i)
                        if r < 2:
                            last = nc.vector.tensor_reduce(nmx[:, m, r, 0:1], ps[b][:, :], AX.X, ALU.max, negate=True)
                        else:
                            last = nc.vector.tensor_reduce(nmx[:, m, r, :], ps[b][:, :].rearrange("p (q k) -> p q k", q=2),
                                                           AX.X, ALU.max, negate=True)
                    last.then_inc(max_done[r], 1)

                def normalise(r):
                    nq = 1 if r < 2 else 2
                    w = TOK // nq
                    names = score_names(kind, L, r)
                    for m, name in enumerate(names):
                        wait_emptied(key, name + s, i)
                    link(nc.vector.reciprocal(rc[:, 0:len(names), r, 0:nq], sm[:, 0:len(names), r, 0:nq]))
                    if kind == "diff":
                        link(nc.vector.tensor_scalar(rc[:, 1, r, 0:nq], rc[:, 1, r, 0:nq], neglam[:, L:L + 1], None, ALU.mult))
                    for t in range(nq):
                        p0 = probs[:, 0, r, w * t:w * t + w]
                        last = nc.vector.tensor_scalar(p0, p0, rc[:, 0, r, t:t + 1], None, ALU.mult)
                    if kind == "diff":
                        link(last)
                        for t in range(nq):
                            p0, p1 = (probs[:, m, r, w * t:w * t + w] for m in (0, 1))
                            last = nc.vector.scalar_tensor_tensor(out=p0, in0=p1, scalar=rc[:, 1, r, t:t + 1], in1=p0,
                                                                  op0=ALU.mult, op1=ALU.add)
                    last.then_inc(norm_done[r], 1)

                if kind == "mla":
                    rope(key, "rot" + s, i, qr[0:64, None, LAT], slice(0, 64))
                    values()
                    split_lo(tq.ahead(2))
                else:
                    split_lo(tq.ahead(2))
                    split_lo(tq.ahead(3))
                    if kind == "diff":
                        rope(key, "rot" + s, i, qk[:, :, LAT], slice(0, P))
                for r in row_groups(L):
                    maxima(r)
                for r in row_groups(L):
                    normalise(r)
                if kind != "mla":
                    values()
                    split_lo(tq.ahead(4))
                if kind == "diff":
                    b = wait_filled(key, "ss" + s, i)
                    nc.vector.tensor_scalar(rs[:, Q], ps[b][:, Q], 1.0 / P, EPS, ALU.mult, ALU.add).then_inc(dms_ready, 1)
                    dve.wait_ge(droot_ready, D_no + 1)
                    nc.vector.reciprocal(rs[:, Q], rs[:, Q]).then_inc(emptied[b], 1)
                    dve.wait_ge(emptied[b], banks.before(key, "ss" + s, i) + 1)
                split_lo(tg.ahead(2))
                wait_emptied(key, "g" + s, i)
                link(nc.vector.tensor_scalar(ge[:, Q], ge[:, Q], 1.0, None, ALU.add))
                link(nc.vector.reciprocal(ge[:, Q], ge[:, Q]))
                link(nc.vector.tensor_tensor(gs[:, Q], gs[:, Q], ge[:, Q], ALU.mult))
                y = Z[:, y_at, Q].rearrange("p o t -> p (o t)")
                if kind == "diff":
                    link(nc.vector.tensor_tensor(gs[:, Q], gs[:, Q], rs[:, Q], ALU.mult))
                    b, bank = bank_of(key, "o" + s)
                    nc.vector.scalar_tensor_tensor(out=y, in0=bank[:, Q], scalar=subc[:, L:L + 1], in1=gs[:, Q],
                                                   op0=ALU.mult, op1=ALU.mult).then_inc(emptied[b], 1)
                else:
                    b = wait_filled(key, "o" + s, i)
                    nc.vector.tensor_tensor(y, ps[b][:, Q], gs[:, Q], ALU.mult).then_inc(emptied[b], 1)

            for L in range(LAYERS):
                key = ("pre", L)
                Q = qcols(L)
                begin()

                def ahead(t):
                    split_lo(Tile(first[L] + t + 2))

                if L == 0:
                    modulate(0, slice(0, TOK), (0, 1))
                    ahead(0)
                    ahead(1)
                else:
                    ahead(0)
                    rstd_of(("post", 0), "ssy", D, slice(0, CTX))
                    new_residual(slice(0, CTX), 2)
                    ahead(1)
                    n["xsq"] += KT + 1
                    dve.wait_ge(sq_used, n["xsq"])
                    n["xsq"] -= 1
                    rstd_of(key, "ssx1", D, slice(0, CTX))
                    modulate(1, slice(0, CTX), (0,))
                for t in range(2, PRE_TILES):
                    ahead(t)
                for name, nt, raws, dsth, dstl, v0 in (("ssq", 4, cqraw, cqh, cql, V_QN + 4 * L), ("sskv", 2, kvraw, kvh, kvl, V_KVN + 2 * L)):
                    cols = Q if name == "ssq" else slice(0, TOK)
                    n["xsq"] += nt
                    dve.wait_ge(sq_used, n["xsq"])
                    rstd_of(key, name, P * nt, cols)
                    for t in range(nt):
                        nc.vector.scalar_tensor_tensor(out=tmp[:, t % 2, cols], in0=raws[:, t, cols], scalar=vcol[:, v0 + t:v0 + t + 1],
                                                       in1=rs[:, cols], op0=ALU.mult, op1=ALU.mult).then_inc(cnorm, 1)
                        n["c"] += 1
                        dve.wait_ge(chi, n["c"])
                        nc.vector.tensor_tensor(dstl[:, t, cols], tmp[:, t % 2, cols], dsth[:, t, cols].bitcast(F32), ALU.subtract).then_inc(clo, 1)
                rope(key, "rot", 0, kr[0:64, None, LAT], slice(0, 64))
                dve.wait_ge(roped, ropes * L + 1)
                end()
                i_links = LINKS[("mla", L)]
                with dve.Fori(0, MLA_H // 2) as i:
                    begin(i, i_links)
                    for j in range(2):
                        tq = Tile(mla0[L] + 2 * j, i)
                        head("mla", L, i, j, tq, tq.ahead(1), HEADS * L + j + 2 * i, bass.ds(2 * i + j, 1), None)
                end(MLA_H // 2)
                with dve.Fori(0, NA_H) as i:
                    begin(i, LINKS[("na", L)])
                    tq = Tile(na0[L], i)
                    head("na", L, i, 0, tq, tq.ahead(3), HEADS * L + MLA_H + i, bass.ds(MLA_H + i, 1), None)
                end(NA_H)
                with dve.Fori(0, DIFF_H) as i:
                    begin(i, LINKS[("diff", L)])
                    tq = Tile(diff0[L], i)
                    head("diff", L, i, 0, tq, tq.ahead(3), HEADS * L + MLA_H + NA_H + i, bass.ds(MLA_H + NA_H + i, 1), DIFF_H * L + i)
                end(DIFF_H)
                for t in range(KT):
                    dve.wait_ge(yhi, L * KT + t + 1)
                    nc.vector.tensor_tensor(hl[:, t, Q], Z[:, t, Q], hh[:, t, Q].bitcast(F32), ALU.subtract).then_inc(ylo, 1)

                def out_tile(i, k, ahead):
                    dve.wait_ge(ysq_ready, n["ysq"] + 4 * i + k + 1)
                    if isinstance(i, int) and i == 0 and k == 0:
                        nc.vector.tensor_copy(acc[:, Q], sq[0][:, Q]).then_inc(acc_ready, 1)
                    else:
                        dve.wait_ge(acc_ready, n["ysq"] + 4 * i + k)
                        nc.vector.tensor_tensor(acc[:, Q], acc[:, Q], sq[k % 2][:, Q], ALU.add).then_inc(acc_ready, 1)
                    if ahead:
                        split_lo(Tile(out0[L] + k, i).ahead(2))

                for k in range(4):
                    out_tile(0, k, True)
                with dve.Fori(1, KT // 4 - 1) as i:
                    for k in range(4):
                        out_tile(i, k, True)
                for k in range(4):
                    out_tile(KT // 4 - 1, k, not (L == LAYERS - 1 and k >= 2))
                n["ysq"] += KT
                begin()
                b = wait_filled(("post", L), "ssy")
                if L < LAYERS - 1:
                    rstd(ps[b][:, LAT], D, LAT)
                else:
                    rstd_of(("post", L), "ssy", D, LAT)
                for b in (0, 1):
                    dve.wait_ge(emptied[b], banks.before(("out", L), f"y{2 + b}", KT // 4 - 1) + 1)
                new_residual(LAT, 2 * L + 1)
                if L < LAYERS - 1:
                    n["xsq"] += KT
                    dve.wait_ge(sq_used, n["xsq"])
                    rstd_of(("pre", L + 1), "ssx0", D, LAT)
                    modulate(L + 1, LAT, (1,))
                end()

        @block.tensor
        def _(pe):
            def claim(key, name, i=0):
                b = banks.bank(key, name)
                u = banks.before(key, name, i)
                if not isinstance(u, int) or u > 0:
                    pe.wait_ge(emptied[b], u)
                return b, ps[b]

            def wait_emptied(key, name, i=0):
                b = banks.bank(key, name)
                pe.wait_ge(emptied[b], banks.before(key, name, i) + 1)

            def mm3(out_ap, w, slot_, c0, cols_w, xh, xl, k, tok, start, stop):
                a, b = wh[:, slot_, c0:c0 + cols_w], wl[:, slot_, c0:c0 + cols_w]
                nc.tensor.matmul(out_ap, a, xh[:, k, tok], start=start, stop=False)
                nc.tensor.matmul(out_ap, a, xl[:, k, tok], start=False, stop=False)
                return nc.tensor.matmul(out_ap, b, xh[:, k, tok], start=False, stop=stop)

            def project(bank, t, tok, k0=0, k1=KT):
                for k in range(k0, k1):
                    last = mm3(bank[:, tok], None, t.split, P * k, P, hh, hl, k, tok, k == 0, k == KT - 1)
                return last

            pe.wait_ge(tab_loaded, 16)
            pe.wait_ge(vec_loaded, 16 * 7)
            nc.tensor.transpose(ps[0][:, 0:V_N], vrows[:, :], ident[0:V_N, 0:V_N]).then_inc(filled[0], 1)
            pe.wait_ge(x_loaded, 32)
            for d in range(KT):
                b, bank = claim("x", f"x{d}")
                for blk in range(4):
                    last = nc.tensor.transpose(bank[:, P * blk:P * blk + P], xin[:, blk, P * d:P * d + P], ident)
                last.then_inc(filled[b], 1)
            items = dict(xsq=0)

            def add_squares(bank, cols, first_one, last_one):
                k = items["xsq"]
                pe.wait_ge(xsq_ready, k + 1)
                nc.tensor.matmul(bank[:, cols], ones, sqx[:, k % 3, cols], start=first_one, stop=last_one).then_inc(sq_used, 1)
                items["xsq"] = k + 1

            b, bank = claim("sumx", "ssx0")
            for d in range(KT):
                add_squares(bank, slice(0, TOK), d == 0, d == KT - 1)
            pe.wait_ge(c_ready, 1)
            for L in range(LAYERS):
                with pe.Fori(0, ADA_UNITS // 2) as i:
                    for j in range(2):
                        b, bank = claim(("ada", L), f"row{j}", i)
                        for t in range(4):
                            tl = Tile(ada0[L] + 4 * j + t, i, 8)
                            pe.wait_ge(lo_done, tl.n + 1)
                            for kk in range(4):
                                k = 4 * t + kk
                                st = cst[:, 4 * k:4 * k + P]
                                nc.tensor.matmul(bank[:, :], st, wh[:, tl.split, 512 * kk:512 * kk + 512], start=(k == 0), stop=False)
                                last = nc.tensor.matmul(bank[:, :], st, wl[:, tl.split, 512 * kk:512 * kk + 512], start=False, stop=(k == KT - 1))
                            last.then_inc(tile_used, 1)
                        wait_emptied(("ada", L), f"row{j}", i)
                        pe.wait_ge(brow_loaded[j], 16 * (L * ADA_UNITS // 2 + 1) + 16 * i)
                        b, bank = claim(("ada", L), f"col{j}", i)
                        for u in range(4):
                            last = nc.tensor.matmul(bank[:, 2 * u:2 * u + 2], arow[:, j, P * u:P * u + P], sel, start=True, stop=True)
                        last.then_inc(filled[b], 1)

            def head(kind, L, i, j, tq, tg, H, NA_no, rope_no, D_no):
                key, s = (kind, L), str(j)
                Q = qcols(L)
                allt = slice(0, TOK)
                if kind == "mla":
                    pe.wait_ge(lo_done, tq.n + 1)
                    sl = tq.split
                    for name, c0, nk, xh, xl, tok, step_c in (("qn", 0, 4, cqh, cql, Q, 192), ("qr", 128, 4, cqh, cql, Q, 192),
                                                              ("kn", 768, 2, kvh, kvl, allt, 256), ("v", 768 + 128, 2, kvh, kvl, allt, 256)):
                        b, bank = claim(key, name + s, i)
                        for k in range(nk):
                            last = mm3(bank[:, tok], None, sl, c0 + step_c * k, P, xh, xl, k, tok, k == 0, k == nk - 1)
                        last.then_inc(tile_used if name == "v" else filled[b], 1)
                else:
                    for k, (name, tok) in enumerate((("q", Q), ("k", allt))):
                        tl = tq.ahead(k)
                        pe.wait_ge(lo_done, tl.n + 1)
                        b, bank = claim(key, name + s, i)
                        project(bank, tl, tok).then_inc(tile_used, 1)
                    tv = tq.ahead(2)
                    pe.wait_ge(lo_done, tv.n + 1)
                    _, vbank = claim(key, "v" + s, i)
                    project(vbank, tv, allt, 0, 6)

                def gate(k0, k1):
                    if k0 == 0:
                        pe.wait_ge(lo_done, tg.n + 1)
                        claim(key, "g" + s, i)
                    last = project(ps[banks.bank(key, "g" + s)], tg, Q, k0, k1)
                    if k1 == KT:
                        last.then_inc(tile_used, 1)

                def turn_values():
                    wait_emptied(key, "v" + s, i)
                    b, bank = claim(key, "vn" + s, i)
                    for kt in range(4):
                        last = nc.tensor.transpose(bank[:, P * kt:P * kt + P], vT[:, P * kt:P * kt + P], ident)
                    last.then_inc(filled[b], 1)

                if kind == "mla":
                    gate(0, 4)
                    wait_emptied(key, "qr" + s, i)
                    b, bank = claim(key, "rot" + s, i)
                    nc.tensor.matmul(bank[:, 0:256], rotm[0:64, :], qr[0:64, LAT], start=True, stop=True).then_inc(filled[b], 1)
                    turn_values()
                    gate(4, 8)
                elif kind == "diff":
                    wait_emptied(key, "q" + s, i)
                    wait_emptied(key, "k" + s, i)
                    b, bank = claim(key, "rot" + s, i)
                    nc.tensor.matmul(bank[:, 0:256], rotm, qk[:, 0, LAT], start=True, stop=True)
                    nc.tensor.matmul(bank[:, 256:512], rotm, qk[:, 1, LAT], start=True, stop=True).then_inc(filled[b], 1)
                if kind != "mla":
                    project(vbank, tv, allt, 6, 12)
                if kind == "na":
                    wait_emptied(key, "q" + s, i)
                    wait_emptied(key, "k" + s, i)
                    pe.wait_ge(bias_built, NA_no + 1)
                elif kind == "mla":
                    wait_emptied(key, "qn" + s, i)
                    wait_emptied(key, "kn" + s, i)
                    pe.wait_ge(roped, rope_no)
                else:
                    pe.wait_ge(roped, rope_no)
                names = [nm for r in row_groups(L) for nm in score_names(kind, L, r)]
                for x_, name in enumerate(names):
                    r = 2 if "ctx" in name else int(name[5])
                    b, bank = claim(key, name + s, i)
                    parts = [(P * 2 + P * r, slice(0, TOK), bank[:, :])] if r < 2 else [
                        (P * t, slice(0, CTX), bank[:, CTX * t:CTX * t + CTX]) for t in range(2)]
                    for q0, keys, dst in parts:
                        if kind == "diff":
                            rows = slice(0, 64) if name[-1] == "a" else slice(64, 128)
                            last = nc.tensor.matmul(dst, qk[rows, 0, q0:q0 + P], qk[rows, 1, keys], start=True, stop=True)
                        elif kind == "mla":
                            nc.tensor.matmul(dst, qk[:, 0, q0:q0 + P], qk[:, 1, keys], start=True, stop=False)
                            last = nc.tensor.matmul(dst, qr[0:64, q0:q0 + P], kr[0:64, keys], start=False, stop=True)
                        elif r < 2:
                            nc.tensor.matmul(dst, qk[:, 0, q0:q0 + P], qk[:, 1, keys], start=True, stop=False)
                            w0 = GRID_W * (2 - 2 * r)
                            last = nc.tensor.matmul(bank[:, LAT], rev, btm[:, w0:w0 + SEQ], start=False, stop=True)
                        else:
                            last = nc.tensor.matmul(dst, qk[:, 0, q0:q0 + P], qk[:, 1, keys], start=True, stop=True)
                    last.then_inc(filled[b], 1)
                    if kind == "diff" and x_ == 2:
                        project(vbank, tv, allt, 12, 14)
                if kind == "mla":
                    gate(8, 14)
                else:
                    project(vbank, tv, allt, 14 if kind == "diff" else 12, KT).then_inc(tile_used, 1)
                    gate(0, 4)
                    turn_values()
                for r in row_groups(L):
                    pe.wait_ge(norm_done[r], H + 1)
                    b, bank = claim(key, ("pt_lat0", "pt_lat1", "pt_ctx")[r] + s, i)
                    if r < 2:
                        for kt in range(4):
                            last = nc.tensor.transpose(bank[:, P * kt:P * kt + P], probs[:, 0, r, P * kt:P * kt + P], ident)
                    else:
                        for kt in range(2):
                            for t in range(2):
                                last = nc.tensor.transpose(bank[:, CTX * kt + P * t:CTX * kt + P * t + P],
                                                           probs[:, 0, r, CTX * t + P * kt:CTX * t + P * kt + P], ident)
                    last.then_inc(filled[b], 1)
                if kind == "mla":
                    gate(14, KT)
                else:
                    gate(4, 8)
                wait_emptied(key, "vn" + s, i)
                for r in row_groups(L):
                    wait_emptied(key, ("pt_lat0", "pt_lat1", "pt_ctx")[r] + s, i)
                b, bank = claim(key, "o" + s, i)
                if L == 0:
                    for kt in range(2):
                        nc.tensor.matmul(bank[:, 0:CTX], vN[:, kt, :], ptc[:, kt, :], start=(kt == 0), stop=(kt == 1))
                for kt in range(4):
                    last = nc.tensor.matmul(bank[:, LAT], vN[:, kt, :], ptl[:, kt, :], start=(kt == 0), stop=(kt == 3))
                last.then_inc(filled[b], 1)
                if kind == "diff":
                    gate(8, 12)
                    pe.wait_ge(dsq_ready, D_no + 1)
                    b, bank = claim(key, "ss" + s, i)
                    nc.tensor.matmul(bank[:, Q], ones, sq[1][:, Q], start=True, stop=True).then_inc(filled[b], 1)
                    gate(12, KT)
                elif kind == "na":
                    gate(8, KT)

            for L in range(LAYERS):
                key = ("pre", L)
                Q = qcols(L)
                allt = slice(0, TOK)

                def pre_tile(t):
                    tl = Tile(first[L] + t)
                    pe.wait_ge(lo_done, tl.n + 1)
                    b, bank = claim(key, f"t{t}")
                    tok = Q if t < 4 else allt
                    if t == 0 or (L == 1 and t == 4):
                        for k in range(KT):
                            pe.wait_ge(hlo, (KT * L if t == 0 else 2 * KT) + k + 1)
                            last = project(bank, tl, tok, k, k + 1)
                    elif L == 1 and t == 1:
                        _, sbank = claim(key, "ssx1")
                        for k in range(KT):
                            last = project(bank, tl, tok, k, k + 1)
                            if k == KT - 1:
                                last.then_inc(tile_used, 1)
                            if k == 0:
                                sums(0)
                            add_squares(sbank, slice(0, CTX), k == 0, k == KT - 1)
                    else:
                        last = project(bank, tl, tok)
                    if not (L == 1 and t == 1):
                        last.then_inc(tile_used, 1)
                    if t and not (L == 1 and t == 1):
                        sums(t - 1)

                def sums(t):
                    if t < 6:
                        name = "ssq" if t < 4 else "sskv"
                        if t in (0, 4):
                            claim(key, name)
                        add_squares(ps[banks.bank(key, name)], Q if t < 4 else allt, t in (0, 4), t in (3, 5))

                if L == 1:
                    b, bank = claim(key, "ssx0")
                    for k in range(KT):
                        add_squares(bank, LAT, k == 0, k == KT - 1)
                for t in range(PRE_TILES):
                    pre_tile(t)
                wait_emptied(key, "t6")
                b, bank = claim(key, "rot")
                nc.tensor.matmul(bank[:, 0:256], rotm[0:64, :], kr[0:64, LAT], start=True, stop=True).then_inc(filled[b], 1)
                pe.wait_ge(clo, 6 * (L + 1))
                with pe.Fori(0, MLA_H // 2) as i:
                    for j in range(2):
                        tq = Tile(mla0[L] + 2 * j, i)
                        head("mla", L, i, j, tq, tq.ahead(1), HEADS * L + j + 2 * i, None, ropes * L + 2 + j + 2 * i, None)
                with pe.Fori(0, NA_H) as i:
                    tq = Tile(na0[L], i)
                    head("na", L, i, 0, tq, tq.ahead(3), HEADS * L + MLA_H + i, NA_H * L + i, None, None)
                with pe.Fori(0, DIFF_H) as i:
                    tq = Tile(diff0[L], i)
                    head("diff", L, i, 0, tq, tq.ahead(3), HEADS * L + MLA_H + NA_H + i, None, ropes * L + MLA_H + 2 + i, DIFF_H * L + i)

                def out_tile(i, k):
                    tl = Tile(out0[L] + k, i)
                    pe.wait_ge(lo_done, tl.n + 1)
                    b, bank = claim(("out", L), f"y{k}", i)
                    if isinstance(i, int) and k == 0:
                        for kk in range(KT):
                            pe.wait_ge(ylo, L * KT + kk + 1)
                            last = project(bank, tl, Q, kk, kk + 1)
                    else:
                        last = project(bank, tl, Q)
                    last.then_inc(tile_used, 1)

                for k in range(4):
                    out_tile(0, k)
                with pe.Fori(1, KT // 4) as i:
                    for k in range(4):
                        out_tile(i, k)
                pe.wait_ge(acc_ready, KT * (L + 1))
                b, bank = claim(("post", L), "ssy")
                nc.tensor.matmul(bank[:, Q], ones, acc[:, Q], start=True, stop=True).then_inc(filled[b], 1)
            for g in range(8):
                q, blk = g // 2, g % 2
                b, bank = claim("final", f"o{g}")
                pe.wait_ge(xnew, 2 * KT * (LAYERS - 1) + 4 * q + 4)
                for dd in range(4):
                    t0 = CTX + P * blk
                    last = nc.tensor.transpose(bank[:, P * dd:P * dd + P], Z[:, 4 * q + dd, t0:t0 + P], ident)
                last.then_inc(filled[b], 1)


DIFF_QK_ = ROT
LINKS = {("mla", 0): 14, ("mla", 1): 12, ("na", 0): 6, ("na", 1): 5, ("diff", 0): 14, ("diff", 1): 11}


def ada_src(w_ada, L, quarter, col):
    v = w_ada[L].rearrange("(k p) n -> p k n", p=P)
    return v[:, 4 * quarter:4 * quarter + 4, bass.ds(col, 512)] if not isinstance(col, int) else v[:, 4 * quarter:4 * quarter + 4, col:col + 512]


_INS = ["x", "c", "ctx", "c_ctx", "w_ada", "b_ada", "norm_pre", "norm_post", "w_in", "mla_q_norm", "mla_kv_norm",
        "w_uq", "w_ukv", "na_rpb", "diff_lq1", "diff_lk1", "diff_lq2", "diff_lk2", "diff_subln", "w_out"]
_OUTS = [((1, SEQ, D), "float32")]


def kernel(**inputs):
    import numpy as _np
    import concourse.bacc as _bacc
    from concourse import mybir as _mybir
    from concourse.bass_utils import run_bass_kernel_spmd as _run

    nc = _bacc.Bacc("TRN2", target_bir_lowering=False, num_devices=1)
    arrays = {"in_table_dram": tables()}
    args = [nc.dram_tensor("in_table_dram", (P, T_W), _mybir.dt.float32, kind="ExternalInput").ap()]
    for name in _INS:
        a = _np.ascontiguousarray(inputs[name])
        arrays[f"in_{name}_dram"] = a
        args.append(nc.dram_tensor(f"in_{name}_dram", a.shape, _mybir.dt.from_np(a.dtype), kind="ExternalInput").ap())
    for i, (shape, dtype) in enumerate(_OUTS):
        dt = _mybir.dt.from_np(_np.dtype(dtype))
        args.append(nc.dram_tensor(f"out_{i}_dram", shape, dt, kind="ExternalOutput").ap())
    backbone(nc, *args)
    r = _run(nc, [arrays], core_ids=[0])
    got = tuple(r.results[0][f"out_{i}_dram"] for i in range(len(_OUTS)))
    return got[0]
```

```python
import math
from contextlib import ExitStack

import numpy as np
import concourse.bass as bass
from concourse import mybir

F32 = mybir.dt.float32
F32R = mybir.dt.float32r
ALU = mybir.AluOpType
ACT = mybir.ActivationFunctionType
AX = mybir.AxisListType

P = 128
D = 2048
KT = D // P
CTX = 256
SEQ = 256
TOK = CTX + SEQ
LAT = slice(CTX, TOK)
LAYERS = 2
GRID_W = 64
ROT = 64
THETA = 10000.0
EPS = 1e-6
MLA_H, NA_H, DIFF_H = 6, 5, 5
HEADS = MLA_H + NA_H + DIFF_H
NOPE, ROPE = 128, 64
Q_RANK, KV_RANK = 512, 256
RPB_R, RPB_C = 15, 31
WIN_W = 16
NEG = -1.0e30

C_CKV = Q_RANK
C_KR = C_CKV + KV_RANK
C_NA = C_KR + ROPE
C_DIFF = C_NA + 3 * NA_H * P
C_G = C_DIFF + 3 * DIFF_H * P

T_ID, T_REV, T_ROT, T_ONE = 0, 128, 256, 384
T_COS, T_SIN, T_MASK, T_SEL = 512, 768, 1024, 1088
T_W = 1090

V_C, V_PRE, V_POST, V_QN, V_KVN, V_SUB, V_N = 0, 32, 64, 96, 104, 108, 110

ADA_UNITS = 3 * D // 512
ADA_FIRST = 2 * D // 512
START_TILES = 4 * ADA_FIRST
LATE = LAYERS * ADA_UNITS - ADA_FIRST
HALVES = 8
PRE_TILES = 7
LAYER_TILES = PRE_TILES + 2 * MLA_H + 4 * NA_H + 4 * DIFF_H + KT


def tables():
    t = np.zeros((P, T_W), np.float32)
    t[:, T_ID:T_ID + P] = np.eye(P, dtype=np.float32)
    for p in range(P):
        t[p, T_REV + 64 * (p // 64) + 63 - p % 64] = 1.0
    q = ROT // 4
    for b in range(2):
        for i in range(ROT):
            src, sign = (i + q, -1.0) if (i // q) % 2 == 0 else (i - q, 1.0)
            t[64 * b + src, T_ROT + 64 * b + i] = sign
    t[:, T_ONE:T_ONE + P] = 1.0
    n = np.arange(SEQ)
    half = ROT // 2
    inv = (1.0 / (np.float32(THETA) ** (np.arange(0, half, 2, dtype=np.float32) / np.float32(half)))).astype(np.float32)
    ar = (n // GRID_W).astype(np.float32)[:, None] * inv[None]
    ac = (n % GRID_W).astype(np.float32)[:, None] * inv[None]
    ang = np.concatenate([ar, ar, ac, ac], axis=-1).astype(np.float32).T
    t[:, T_COS:T_COS + SEQ] = np.tile(np.cos(ang), (2, 1))
    t[:, T_SIN:T_SIN + SEQ] = np.tile(np.sin(ang), (2, 1))
    for p in range(P):
        qc = 63 - p % 64
        lo = min(max(qc - WIN_W // 2, 0), GRID_W - WIN_W)
        t[p, T_MASK:T_MASK + GRID_W] = NEG
        t[p, T_MASK + lo:T_MASK + lo + WIN_W] = 0.0
    t[0:2, T_SEL] = 1.0
    t[2:4, T_SEL + 1] = 1.0
    return t


class Tile:

    def __init__(self, first, i=0, per=4):
        self.n = first + per * i
        self.split = first % 2
        if first < START_TILES:
            self.raw, self.round = first % 4, first // 4 + (per // 4) * i
        else:
            self.raw, self.round = first % 2, START_TILES // 4 + (first - START_TILES) // 2 + (per // 2) * i
        self.first, self.i, self.per = first, i, per

    def ahead(self, k):
        return Tile(self.first + k, self.i, self.per)


class Banks:

    def __init__(self, phases):
        self.plan = {}
        fills, uses = [0] * 8, [0] * 8
        for key, trips, groups in phases:
            step_f, step_u = [0] * 8, [0] * 8
            at = {}
            for name, b, by_tile in groups:
                at[name] = (b, step_u[b], step_f[b])
                step_u[b] += 1
                step_f[b] += not by_tile
            self.plan[key] = (list(uses), list(fills), step_u, step_f, at)
            for b in range(8):
                uses[b] += trips * step_u[b]
                fills[b] += trips * step_f[b]

    def bank(self, key, name):
        return self.plan[key][4][name][0]

    def before(self, key, name, i=0):
        uses, _, step, _, at = self.plan[key]
        b, u, _ = at[name]
        return uses[b] + u + step[b] * i

    def filled(self, key, name, i=0):
        _, fills, _, step, at = self.plan[key]
        b, _, f = at[name]
        return fills[b] + f + 1 + step[b] * i


def head_groups(kind, L, j=0):
    s = str(j)
    ac = [("ac" + s, 5, True)] if L == 0 and j == 0 else []
    if kind == "mla":
        a, b = (0, 1) if j == 0 else (1, 0)
        g = ac + [("qn" + s, a, False), ("qr" + s, b, False), ("kn" + s, a, False), ("v" + s, b, True),
             ("g" + s, a, True), ("rot" + s, 7, False)]
    else:
        g = ac + [("q" + s, 0, True), ("k" + s, 1, True), ("v" + s, 0, True), ("g" + s, 1, True)]
        if kind == "diff":
            g += [("rot" + s, 7, False)]
    g += [("vn" + s, 5, False)]
    for name, b in score_banks(kind, L):
        g += [(name + s, b, False)]
    g += [("pt_lat0" + s, 6, False), ("pt_lat1" + s, 5, False)]
    if L == 0:
        g += [("pt_ctx" + s, 6, False)]
    g += [("o" + s, 7, False)]
    if kind == "diff":
        g += [("ss" + s, 6, False)]
    return g


def score_banks(kind, L):
    if kind == "diff":
        s = [("s_lat0a", 2), ("s_lat0b", 3), ("s_lat1a", 4), ("s_lat1b", 2)]
        return s + ([("s_ctxa", 3), ("s_ctxb", 4)] if L == 0 else [])
    s = [("s_lat0", 2), ("s_lat1", 3)]
    return s + ([("s_ctx", 4)] if L == 0 else [])


def psum_plan():
    ph = [("vec", 1, [("vt", 0, False)])]
    ph += [("x", 1, [(f"x{d}", 4 + d % 3, False) for d in range(KT)])]
    ph += [("sumx", 1, [("ssx0", 7, True)])]
    ph += [("ada", ADA_FIRST // 2, [("row0", 0, True), ("col0", 2, False), ("row1", 1, True), ("col1", 3, False)])]

    for L in range(LAYERS):
        ph += [(("pre", L), 1, [("ssx0", 2, True), ("ssx1", 3, True)][:2 * L] + [(f"t{t}", t % 2, True) for t in range(PRE_TILES)]
                + [("ssq", 2, True), ("sskv", 3, True), ("rot", 7, False)])]
        ph += [(("mla", L), MLA_H // 2, head_groups("mla", L, 0) + head_groups("mla", L, 1))]
        ph += [(("na", L), NA_H, head_groups("na", L))]
        ph += [(("diff", L), DIFF_H, head_groups("diff", L))]
        ph += [(("out", L), KT // 4, [(f"y{t}", t % 2, True) for t in range(4)])]
        if L == 0:
            ph += [("ada_out", 3, [("ac", 5, True)])]
        ph += [(("post", L), 1, [("ssy", 4, False)])]
    ph += [("final", 1, [(f"o{g}", g, False) for g in range(8)])]
    return Banks(ph)


def backbone(nc, table, x, c, ctx_in, c_ctx, w_ada, b_ada, norm_pre, norm_post, w_in, mla_q_norm, mla_kv_norm,
             w_uq, w_ukv, na_rpb, diff_lq1, diff_lk1, diff_lq2, diff_lk2, diff_subln, w_out, out):
    banks = psum_plan()
    stack = ExitStack()
    with stack:
        sem_names = []

        def sem(name):
            sem_names.append(name)
            return stack.enter_context(nc.semaphore(name))

        base = (nc.sbuf_base + 63) // 64 * 64
        KB = 1024

        def at(name, shape, off, dt=F32):
            return nc.alloc_sbuf_tensor_at(name, shape, dt, offset=base + off)

        Z = at("residual_mixed_out", [P, KT, TOK], 0)
        hh = at("act_hi", [P, KT, TOK], 32 * KB, F32R)
        hl = at("act_lo", [P, KT, TOK], 64 * KB, F32R)
        xin = at("tokens_in", [P, 4, D], 64 * KB)
        oout = at("tokens_out", [P, 2, D], 64 * KB)
        raw = at("w_raw", [P, 4, 2048], 96 * KB)
        araw = at("ada_raw", [P, 2, 1024], 112 * KB)
        aacc = at("ada_sums", [P, 2, 512], 120 * KB)
        wh = at("w_hi", [P, 2, 2048], 128 * KB, F32R)
        wl = at("w_lo", [P, 2, 2048], 144 * KB, F32R)
        cqh = at("cq_hi", [P, 4, TOK], 12 * KB, F32R)
        cql = at("cq_lo", [P, 4, TOK], 20 * KB, F32R)
        kvh = at("ckv_hi", [P, 2, TOK], 28 * KB, F32R)
        off = 160 * KB
        tab = at("tables", [P, T_W], off)
        off += T_W * 4 + 24
        qk = at("qk", [P, 2, TOK], off)
        off += 4 * KB
        vT = at("vT", [P, TOK], off)
        off += 2 * KB
        vN = at("vN", [P, 4, P], off)
        off += 2 * KB
        qr = at("q_rot", [P, TOK], off)
        kr = at("k_rot", [P, TOK], off + 2 * KB)
        xback = at("residual_back", [P, KT, SEQ], off - 8 * KB)
        bt = at("bias_raw", [P, 6 * GRID_W], off)
        btm = at("bias_masked", [P, 6 * GRID_W], off + 2 * KB)
        off += 4 * KB
        probs = at("probs", [P, 2, 3, TOK], off)
        kvraw = at("ckv_raw", [P, 2, TOK], off)
        cqraw = at("cq_raw", [P, 4, TOK], off + 4 * KB)
        kvl = at("ckv_lo", [P, 2, TOK], off + 8 * KB, F32R)
        arow = at("ada_rows", [4, 2, 512], off)
        vrows = at("vec_rows", [V_N, P], off + 4 * KB)
        brows = at("b_ada_rows", [LAYERS * 3 * KT, P], off + 5 * KB)
        off += 12 * KB
        ptl = at("probsT_lat", [P, 4, SEQ], off)
        sqx = at("squares", [P, 3, TOK], off)
        ptc = at("probsT_ctx", [P, 2, CTX], off + 4 * KB)
        off += 6 * KB
        tmp = at("tmp", [P, 4, TOK], off)
        lamr = at("lam_rows", [P, LAYERS * 4, DIFF_QK], off)
        off += 8 * KB
        rs = at("rstd", [P, TOK], off)
        off += 2 * KB
        vcol = at("vec_cols", [P, V_N], off)
        off += 448
        ada = at("ada_cols", [P, LAYERS, 48, 2], off)
        off += 768
        ada_flat = ada.rearrange("p l c s -> p (l c) s")
        A = at("scale_cols", [P, LAYERS, KT, 2], off)
        off += 256
        G = at("gate_cols", [P, LAYERS, KT, 2], off)
        off += 256
        cst = at("c_split", [P, 4 * KT + P], off, F32R)
        off += 768
        stat = at("stats", [P, 48], off)
        off += 192
        warm = at("warm", [P, 8], off)
        off += 32
        scol = at("silu_cols", [P, 2 * KT], off)
        off += 128
        bcol = at("b_ada_cols", [P, LAYERS * 3 * KT], off)
        off += 384
        assert base + off <= nc.sbuf_usable_end
        nmx = stat[:, 0:12].rearrange("p (m r q) -> p m r q", m=2, r=3)
        sm = stat[:, 12:24].rearrange("p (m r q) -> p m r q", m=2, r=3)
        rc = stat[:, 24:36].rearrange("p (m r q) -> p m r q", m=2, r=3)
        neglam = stat[:, 36:38]
        ldot = stat[:, 38:42].rearrange("p (l t) -> p l t", l=2)
        lexp = stat[:, 42:46].rearrange("p (l t) -> p l t", l=2)
        subc = stat[:, 46:48]
        sq = [tmp[:, 0, :], tmp[:, 1, :]]
        acc = tmp[:, 2, :]
        gs, ge = tmp[:, 2, :], tmp[:, 3, :]

        ident = tab[:, T_ID:T_ID + P]
        rev = tab[:, T_REV:T_REV + P]
        rotm = tab[:, T_ROT:T_ROT + P]
        ones = tab[:, T_ONE:T_ONE + P]
        cos = tab[:, T_COS:T_COS + SEQ]
        sin = tab[:, T_SIN:T_SIN + SEQ]
        mask = tab[:, T_MASK:T_MASK + GRID_W]
        sel = tab[0:4, T_SEL:T_SEL + 2]

        ps = [stack.enter_context(nc.psum_tensor(f"bank{b}", [P, 512], F32)) for b in range(8)]
        spill = nc.dram_tensor("residual_spill", [P, KT, TOK], F32, kind="Internal").ap()

        filled = [sem(f"bank_filled{b}") for b in range(8)]
        emptied = [sem(f"bank_emptied{b}") for b in range(8)]
        raw_loaded = [sem(f"raw_loaded{b}") for b in range(4)]
        ukv_loaded = sem("ukv_loaded")
        hi_done = sem("hi_done")
        lo_done = sem("lo_done")
        tile_used = sem("tile_used")
        tab_loaded = sem("tab_loaded")
        vec_loaded = sem("vec_loaded")
        x_loaded = sem("x_loaded")
        lam_loaded = sem("lam_loaded")
        half_loaded = [sem(f"half_loaded{j}") for j in range(2)]
        ada_added = sem("ada_added")
        ada_summed = sem("ada_summed")
        rpb_loaded = sem("rpb_loaded")
        c_exp = sem("c_exp")
        c_ready = sem("c_ready")
        lam_dot = sem("lam_dot")
        lam_exp = sem("lam_exp")
        consts_ready = sem("consts_ready")
        xsq_ready = sem("xsq_ready")
        ysq_ready = sem("ysq_ready")
        acc_ready = sem("acc_ready")
        ms_ready = sem("ms_ready")
        warmed = sem("warmed")
        root_ready = sem("root_ready")
        hval = sem("hval")
        sq_used = sem("sq_used")
        ylo = sem("ylo")
        ylo_pool = sem("ylo_pool")
        hhi = sem("hhi")
        yhi = sem("yhi")
        chi = sem("chi")
        hlo = sem("hlo")
        clo = sem("clo")
        cnorm = sem("cnorm")
        roped = sem("roped")
        max_done = [sem(f"max_done_{r}") for r in ("lat0", "lat1", "ctx")]
        norm_done = [sem(f"norm_done_{r}") for r in ("lat0", "lat1", "ctx")]
        dsq_ready = sem("dsq_ready")
        droot_ready = sem("droot_ready")
        bias_built = sem("bias_built")
        spilled = sem("spilled")
        back = sem("back")
        xnew = sem("xnew")
        halfway = sem("halfway")
        dve_chain = sem("dve_chain")
        o_ready = sem("o_ready")
        stored = sem("stored")

        first = [START_TILES + L * LAYER_TILES for L in range(LAYERS)]
        mla0 = [f + PRE_TILES for f in first]
        na0 = [f + 2 * MLA_H for f in mla0]
        diff0 = [f + 4 * NA_H for f in na0]
        out0 = [f + 4 * DIFF_H for f in diff0]
        last_tile = out0[-1] + KT - 1
        ropes = 1 + MLA_H + DIFF_H
        half = [slice(0, CTX), LAT]
        stream = [1, 0]

        def qcols(L):
            return slice(0, TOK) if L == 0 else LAT

        def act_halves(L):
            return (1, 0) if L == 0 else (1,)

        def mod_groups(L):
            return [(slice(0, TOK), (0, 1))] if L == 0 else [(LAT, (1,)), (slice(0, CTX), (0,))]

        mod0 = [0, KT]

        def row_groups(L):
            return (0, 1, 2) if L == 0 else (0, 1)

        def score_names(kind, L, r):
            nm = ("s_lat0", "s_lat1", "s_ctx")[r]
            return [nm + "a", nm + "b"] if kind == "diff" else [nm]

        def late_unit(kind, i=0):
            return {"pre": (0, 0, ADA_FIRST), "mla": (i + 1, 0, i + ADA_FIRST + 1), "na": (i + 4, 1, i),
                    "diff": (i + 9, 1, i + 5), "out": (i + 13, 1, i + 9)}[kind]

        block = stack.enter_context(nc.Block())

        @block.sync
        def _(sp):
            def load(t, src, dst):
                if t.first >= START_TILES + 2:
                    sp.wait_ge(lo_done, t.n - 1)
                elif t.first >= 4 or not isinstance(t.n, int):
                    sp.wait_ge(lo_done, t.n - 3)
                sp.dma_start(dst, src).then_inc(raw_loaded[t.raw], 16)

            def slot(t, c):
                return raw[:, t.raw, :].rearrange("p (k c) -> p k c", c=c)

            def w_cols(w, L, col):
                return w[L].rearrange("(k p) n -> p k n", p=P)[:, :, col]

            sp.dma_start(xin[:, 0:2, :], ctx_in[0].rearrange("(b p) d -> p b d", p=P)).then_inc(x_loaded, 16)
            sp.dma_start(xin[:, 2:4, :], x[0].rearrange("(b p) d -> p b d", p=P)).then_inc(x_loaded, 16)
            sp.dma_start(tab[:, :], table).then_inc(tab_loaded, 16)
            rows = [(V_C, c.rearrange("a (r p) -> (a r) p", p=P)), (V_C + 16, c_ctx.rearrange("(r p) -> r p", p=P)),
                    (V_PRE, norm_pre.rearrange("l (r p) -> (l r) p", p=P)),
                    (V_POST, norm_post.rearrange("l (r p) -> (l r) p", p=P)),
                    (V_QN, mla_q_norm.rearrange("l (r p) -> (l r) p", p=P)),
                    (V_KVN, mla_kv_norm.rearrange("l (r p) -> (l r) p", p=P)), (V_SUB, diff_subln)]
            sp.dma_start(brows[:, :], b_ada.rearrange("l (r p) -> (l r) p", p=P)).then_inc(vec_loaded, 16)
            for r0, src in rows:
                sp.dma_start(vrows[r0:r0 + src.shape[0], :], src).then_inc(vec_loaded, 16)
            for L in range(LAYERS):
                for k, v in enumerate((diff_lq1, diff_lk1, diff_lq2, diff_lk2)):
                    src = bass.AP(v.tensor, L * DIFF_QK, [[0, P], [1, DIFF_QK]])
                    sp.dma_start(lamr[:, 4 * L + k, :], src).then_inc(lam_loaded, 16)
            for t in range(4):
                load(Tile(t), ada_src(w_ada, 0, t, 0), slot(Tile(t), 512))

            for t in range(4):
                load(Tile(4 + t), ada_src(w_ada, 0, t, D), slot(Tile(4 + t), 512))
            with sp.Fori(1, ADA_FIRST // 2) as i:
                for j in range(2):
                    for t in range(4):
                        tl = Tile(4 * j + t, i, 8)
                        load(tl, ada_src(w_ada, 0, t, 512 * i + D * j), slot(tl, 512))

            for L in range(LAYERS):
                for t in range(PRE_TILES):
                    tl = Tile(first[L] + t)
                    load(tl, w_cols(w_in, L, slice(P * t, P * t + P)), slot(tl, P))
                with sp.Fori(0, MLA_H // 2) as i:
                    for j in range(2):
                        tl = Tile(mla0[L] + 2 * j, i)
                        sp.wait_ge(lo_done, tl.n - 1)
                        uq = w_uq[L].rearrange("(k p) n -> p k n", p=P)[:, :, bass.ds((2 * i + j) * (NOPE + ROPE), NOPE + ROPE)]
                        ukv = w_ukv[L].rearrange("(k p) n -> p k n", p=P)[:, :, bass.ds((2 * i + j) * 256, 256)]
                        sp.dma_start(raw[:, tl.raw, 768:1280].rearrange("p (k c) -> p k c", c=256), ukv).then_inc(ukv_loaded, 16)
                        sp.wait_ge(ukv_loaded, 16 * (L * MLA_H + j + 1) + 32 * i)
                        sp.dma_start(raw[:, tl.raw, 0:768].rearrange("p (k c) -> p k c", c=192), uq).then_inc(raw_loaded[tl.raw], 16)
                        tg = tl.ahead(1)
                        load(tg, w_cols(w_in, L, bass.ds(C_G + P * (2 * i + j), P)), slot(tg, P))
                with sp.Fori(0, NA_H) as i:
                    tl = Tile(na0[L], i)
                    for k, col in enumerate((C_NA, C_NA + NA_H * P, C_NA + 2 * NA_H * P, C_G + MLA_H * P)):
                        load(tl.ahead(k), w_cols(w_in, L, bass.ds(col + P * i, P)), slot(tl.ahead(k), P))
                    sp.wait_ge(tile_used, tl.n + 1)
                    for s in range(2):
                        src = bass.AP(na_rpb.tensor, L * NA_H * RPB_R * RPB_C + (5 - s) * RPB_C - 48 + i * (RPB_R * RPB_C),
                                      [[1, 64], [RPB_C, 6], [1, GRID_W]])
                        dst = bt[64 * s:64 * s + 64, :].rearrange("p (r c) -> p r c", c=GRID_W)
                        sp.dma_start(dst, src).then_inc(rpb_loaded, 16)
                with sp.Fori(0, DIFF_H) as i:
                    tl = Tile(diff0[L], i)
                    for k, col in enumerate((C_DIFF, C_DIFF + DIFF_H * P, C_DIFF + 2 * DIFF_H * P, C_G + (MLA_H + NA_H) * P)):
                        load(tl.ahead(k), w_cols(w_in, L, bass.ds(col + P * i, P)), slot(tl.ahead(k), P))
                with sp.Fori(0, KT // 4) as i:
                    for k in range(4):
                        tl = Tile(out0[L] + k, i)
                        load(tl, w_cols(w_out, L, bass.ds(4 * P * i + P * k, P)), slot(tl, P))
            for g in range(8):
                q, blk = g // 2, g % 2
                sp.wait_ge(o_ready, g + 1)
                sp.dma_start(out[0, P * blk:P * blk + P, 512 * q:512 * q + 512],
                             oout[:, blk, 512 * q:512 * q + 512]).then_inc(stored, 16)
            sp.wait_ge(stored, 16 * 8)

        @block.gpsimd
        def _(pool):
            def load_half(unit, m):
                number, L, u = unit
                if not isinstance(number, int) or 8 * number + m >= 2:
                    pool.wait_ge(ada_added, 4 * (HALVES * number + m - 1))
                else:
                    pool.wait_ge(lo_done, START_TILES)
                src = w_ada[L].rearrange("(k p) n -> p k n", p=P)[:, 2 * m:2 * m + 2, bass.ds(512 * u, 512)]
                pool.dma_start(araw[:, m % 2, :].rearrange("p (k c) -> p k c", c=512), src).then_inc(half_loaded[m % 2], 16)

            pool.wait_ge(tab_loaded, 16)
            m = 0
            for L in range(LAYERS):
                for cols, _ in mod_groups(L):
                    for t in range(KT):
                        pool.wait_ge(hhi, m + 1)
                        nc.gpsimd.tensor_tensor(hl[:, t, cols], tmp[:, m % 4, cols], hh[:, t, cols].bitcast(F32),
                                                ALU.subtract).then_inc(hlo, 1)
                        m += 1
                if L == 0:
                    for h in range(HALVES):
                        load_half(late_unit("pre"), h)
                    with pool.Fori(0, MLA_H // 2) as i:
                        for h in range(HALVES):
                            load_half(late_unit("mla", i), h)
                with pool.Fori(0, NA_H) as i:
                    if L == 0:
                        for h in range(2):
                            load_half(late_unit("na", i), h)
                    pool.wait_ge(rpb_loaded, 32 * (L * NA_H + 1) + 32 * i)
                    nc.gpsimd.tensor_tensor(btm[:, :].rearrange("p (r c) -> p r c", c=GRID_W),
                                            bt[:, :].rearrange("p (r c) -> p r c", c=GRID_W),
                                            mask[:, None, :].to_broadcast([P, 6, GRID_W]), ALU.add).then_inc(bias_built, 1)
                    if L == 0:
                        for h in range(2, HALVES):
                            load_half(late_unit("na", i), h)
                if L == 0:
                    with pool.Fori(0, DIFF_H) as i:
                        for h in range(HALVES):
                            load_half(late_unit("diff", i), h)
                Q = qcols(L)
                for t in range(POOL_HEADS):
                    pool.wait_ge(yhi, L * KT + t + 1)
                    nc.gpsimd.tensor_tensor(hl[:, t, Q], Z[:, t, Q], hh[:, t, Q].bitcast(F32), ALU.subtract).then_inc(ylo_pool, 1)
                if L == 0:
                    with pool.Fori(1, 3) as i:
                        for h in range(HALVES):
                            load_half(late_unit("out", i), h)

        @block.scalar
        def _(act):
            def bank_of(key, name):
                b = banks.bank(key, name)
                return b, ps[b]

            def wait_filled(key, name, i=0):
                b = banks.bank(key, name)
                act.wait_ge(filled[b], banks.filled(key, name, i))
                return b

            def split_hi(t):
                act.wait_ge(raw_loaded[t.raw], 16 * (t.round + 1))
                if not isinstance(t.n, int) or t.n >= 2:
                    act.wait_ge(tile_used, t.n - 1)
                nc.scalar.activation(wh[:, t.split, :], raw[:, t.raw, :], ACT.Copy).then_inc(hi_done, 1)

            act.wait_ge(tab_loaded, 16)
            act.wait_ge(filled[0], banks.filled("vec", "vt"))
            nc.scalar.activation(tmp[:, 3, 0:32], ps[0][:, 0:32], ACT.Exp, scale=-1.0).then_inc(c_exp, 1)
            act.wait_ge(lam_dot, LAYERS)
            nc.scalar.activation(lexp, ldot, ACT.Exp).then_inc(lam_exp, 1)
            items = dict(xsq=0, ysq=0, root=0, mod=0, ylo=0, c=0, back=0, xnew=0)

            def squares(src, cols):
                k = items["xsq"]
                if k >= 3:
                    act.wait_ge(sq_used, k - 2)
                nc.scalar.activation(sqx[:, k % 3, cols], src, ACT.Square).then_inc(xsq_ready, 1)
                items["xsq"] = k + 1

            def take_root(cols):
                if items["root"]:
                    act.wait_ge(warmed, items["root"])
                nc.scalar.activation(warm[:, 0:1], ones[:, 0:1], ACT.Sqrt).then_inc(warmed, 1)
                items["root"] += 1
                act.wait_ge(ms_ready, items["root"])
                nc.scalar.activation(rs[:, cols], rs[:, cols], ACT.Sqrt).then_inc(root_ready, 1)

            def modulated_hi(cols):
                for t in range(KT):
                    m = items["mod"]
                    act.wait_ge(hval, m + 1)
                    nc.scalar.activation(hh[:, t, cols], tmp[:, m % 4, cols], ACT.Copy).then_inc(hhi, 1)
                    items["mod"] = m + 1

            def new_squares(cols):
                for t in range(KT):
                    items["xnew"] += 1
                    act.wait_ge(xnew, items["xnew"])
                    squares(Z[:, t, cols], cols)

            def ada_step(i, tokens=False):
                for j in range(2):
                    for t in range(4):
                        tl = Tile(4 * j + t, i, 8)
                        if t == 3:
                            act.wait_ge(tile_used, tl.n + 1)
                            b, bank = bank_of("ada", f"row{j}")
                            nc.scalar.activation(arow[0:4, j, :], bank[0:4, :], ACT.Copy).then_inc(emptied[b], 1)
                        split_hi(tl.ahead(2))
                        if tokens:
                            two = (8 * j + 2 * t, 8 * j + 2 * t + 1)
                            b = wait_filled("x", f"x{two[0]}")
                            nc.scalar.activation(Z[:, two[0], :], ps[b][:, :], ACT.Copy).then_inc(emptied[b], 1)
                            for d in two:
                                b = banks.bank("x", f"x{d}")
                                act.wait_ge(emptied[b], banks.before("x", f"x{d}") + 1)
                                squares(Z[:, d, :], slice(0, TOK))

            split_hi(Tile(0))
            split_hi(Tile(1))
            ada_step(0, True)
            act.dma_start(spill, Z[:, :, :]).then_inc(spilled, 16)
            take_root(slice(0, TOK))
            with act.Fori(1, ADA_FIRST // 2) as i:
                ada_step(i)

            def ada_columns(number, key, name):
                act.wait_ge(ada_summed, number + 1)
                b, bank = bank_of(key, name)
                nc.scalar.activation(ada_flat[:, bass.ds(4 * number + 2 * KT, 4), :], bank[:, 0:8].rearrange("p (u s) -> p u s", s=2),
                                     ACT.Copy).then_inc(emptied[b], 1)

            def head(kind, L, i, j, tq, tg, H, D_no):
                key, s = (kind, L), str(j)
                Q = qcols(L)
                scale = {"mla": (NOPE + ROPE) ** -0.5, "na": P ** -0.5, "diff": ROT ** -0.5}[kind]
                def exps(r):
                    act.wait_ge(max_done[r], H + 1)
                    for m, name in enumerate(score_names(kind, L, r)):
                        b, bank = bank_of(key, name + s)
                        if r < 2:
                            nc.scalar.activation(probs[:, m, r, :], bank[:, :], ACT.Exp, bias=nmx[:, m, r, 0:1],
                                                 accum_out=sm[:, m, r, 0:1]).then_inc(emptied[b], 1)
                        else:
                            for t in range(2):
                                e = nc.scalar.activation(probs[:, m, r, 256 * t:256 * t + 256], bank[:, 256 * t:256 * t + 256],
                                                         ACT.Exp, bias=nmx[:, m, r, t:t + 1], accum_out=sm[:, m, r, t:t + 1])
                            e.then_inc(emptied[b], 1)

                if kind == "mla":
                    b = wait_filled(key, "qn" + s, i)
                    nc.scalar.activation(qk[:, 0, Q], ps[b][:, Q], ACT.Copy, scale=scale).then_inc(emptied[b], 1)
                    b = wait_filled(key, "qr" + s, i)
                    nc.scalar.activation(qr[0:64, Q], ps[b][0:64, Q], ACT.Copy, scale=scale).then_inc(emptied[b], 1)
                    b = wait_filled(key, "kn" + s, i)
                    nc.scalar.activation(qk[:, 1, :], ps[b][:, :], ACT.Copy).then_inc(emptied[b], 1)
                    act.wait_ge(tile_used, tq.n + 1)
                    b, bank = bank_of(key, "v" + s)
                    nc.scalar.activation(vT[:, :], bank[:, :], ACT.Copy).then_inc(emptied[b], 1)
                    split_hi(tq.ahead(2))
                    if L == 0 and j == 0:
                        ada_columns(late_unit(kind, i)[0] - 1, key, "ac0")
                    for r in row_groups(L):
                        exps(r)
                else:
                    act.wait_ge(tile_used, tq.n + 1)
                    b, bank = bank_of(key, "q" + s)
                    nc.scalar.activation(qk[:, 0, Q], bank[:, Q], ACT.Copy, scale=scale).then_inc(emptied[b], 1)
                    split_hi(tq.ahead(2))
                    if L == 0:
                        ada_columns(late_unit(kind, i)[0] - 1, key, "ac0")
                    act.wait_ge(tile_used, tq.ahead(1).n + 1)
                    b, bank = bank_of(key, "k" + s)
                    nc.scalar.activation(qk[:, 1, :], bank[:, :], ACT.Copy).then_inc(emptied[b], 1)
                    split_hi(tq.ahead(3))
                    for r in row_groups(L):
                        exps(r)
                    act.wait_ge(tile_used, tq.ahead(2).n + 1)
                    b, bank = bank_of(key, "v" + s)
                    nc.scalar.activation(vT[:, :], bank[:, :], ACT.Copy).then_inc(emptied[b], 1)
                    split_hi(tq.ahead(4))
                for r in row_groups(L):
                    b = wait_filled(key, ("pt_lat0", "pt_lat1", "pt_ctx")[r] + s, i)
                    if r < 2:
                        dst, src = ptl[:, :, P * r:P * r + P], ps[b][:, :].rearrange("p (k q) -> p k q", q=P)
                    else:
                        dst, src = ptc[:, :, :], ps[b][:, :].rearrange("p (k q) -> p k q", q=CTX)
                    nc.scalar.activation(dst, src, ACT.Copy).then_inc(emptied[b], 1)
                if kind == "diff":
                    b = wait_filled(key, "o" + s, i)
                    nc.scalar.activation(sq[1][:, Q], ps[b][:, Q], ACT.Square).then_inc(dsq_ready, 1)
                    act.wait_ge(emptied[6], banks.before(key, "ss" + s, i) + 1)
                    nc.scalar.activation(rs[:, Q], rs[:, Q], ACT.Sqrt).then_inc(droot_ready, 1)
                split_hi(tg.ahead(2))
                b7 = "rot" + s if kind != "na" else "o" + s
                act.wait_ge(emptied[7], banks.before(key, b7, i))
                b, bank = bank_of(key, "g" + s)
                nc.scalar.activation(gs[:, Q], bank[:, Q], ACT.Copy)
                nc.scalar.activation(ge[:, Q], bank[:, Q], ACT.Exp, scale=-1.0).then_inc(emptied[b], 1)

            act.wait_ge(consts_ready, 1)
            for L in range(LAYERS):
                key = ("pre", L)
                Q = qcols(L)

                def pre_tile(t, split=True):
                    tl = Tile(first[L] + t)
                    act.wait_ge(tile_used, tl.n + 1)
                    b, bank = bank_of(key, f"t{t}")
                    if t < 6:
                        cols = Q if t < 4 else slice(0, TOK)
                        dst = cqraw[:, t, cols] if t < 4 else kvraw[:, t - 4, cols]
                        squares(bank[:, cols], cols)
                        nc.scalar.activation(dst, bank[:, cols], ACT.Copy).then_inc(emptied[b], 1)
                    else:
                        nc.scalar.activation(kr[:, :], bank[:, :], ACT.Copy).then_inc(emptied[b], 1)
                    if split:
                        split_hi(tl.ahead(2))

                if L == 0:
                    modulated_hi(slice(0, TOK))
                    pre_tile(0)
                    pre_tile(1)
                else:
                    pre_tile(0, False)
                    new_squares(slice(0, CTX))
                    split_hi(Tile(first[L] + 2))
                    pre_tile(1)
                    take_root(slice(0, CTX))
                    pre_tile(2)
                    modulated_hi(slice(0, CTX))
                for t in range(2 + L, PRE_TILES - 1):
                    pre_tile(t)
                    if t < 4:
                        continue
                    nt, dsth = (4, cqh) if t == 4 else (2, kvh)
                    cols = Q if nt == 4 else slice(0, TOK)
                    take_root(cols)
                    if t == PRE_TILES - 2:
                        pre_tile(t + 1)
                    act.wait_ge(spilled, 16 * (L + 1))
                    for u in range(nt):
                        items["c"] += 1
                        act.wait_ge(cnorm, items["c"])
                        nc.scalar.activation(dsth[:, u, cols], tmp[:, u, cols], ACT.Copy).then_inc(chi, 1)
                with act.Fori(0, MLA_H // 2) as i:
                    for j in range(2):
                        tq = Tile(mla0[L] + 2 * j, i)
                        head("mla", L, i, j, tq, tq.ahead(1), HEADS * L + j + 2 * i, None)
                with act.Fori(0, NA_H) as i:
                    tq = Tile(na0[L], i)
                    head("na", L, i, 0, tq, tq.ahead(3), HEADS * L + MLA_H + i, None)
                with act.Fori(0, DIFF_H) as i:
                    tq = Tile(diff0[L], i)
                    head("diff", L, i, 0, tq, tq.ahead(3), HEADS * L + MLA_H + NA_H + i, DIFF_H * L + i)
                act.wait_ge(filled[7], banks.filled(("diff", L), "o0", DIFF_H - 1))
                act.dma_start(xback[:, :, :], spill[:, :, LAT]).then_inc(back, 16)
                act.wait_ge(tile_used, out0[L])
                for t in range(KT):
                    if t == KT - 2:
                        act.wait_ge(emptied[7], banks.before(("diff", L), "o0", DIFF_H - 2) + 1)
                    if t == KT - 1:
                        act.wait_ge(emptied[7], banks.before(("diff", L), "o0", DIFF_H - 1) + 1)
                    nc.scalar.activation(hh[:, t, Q], Z[:, t, Q], ACT.Copy).then_inc(yhi, 1)

                act.wait_ge(consts_ready, 2 + L)

                def out_tile(i, k, ahead):
                    tl = Tile(out0[L] + k, i)
                    act.wait_ge(tile_used, tl.n + 1)
                    b, bank = bank_of(("out", L), f"y{k}")
                    if not (isinstance(i, int) and 4 * i + k < 2):
                        act.wait_ge(acc_ready, items["ysq"] + 4 * i + k - 1)
                    nc.scalar.activation(sq[k % 2][:, Q], bank[:, Q], ACT.Square).then_inc(ysq_ready, 1)
                    for a in act_halves(L):
                        g = G[:, L, bass.ds(4 * i + k, 1), stream[a]:stream[a] + 1].rearrange("p o s -> p (o s)")
                        last = nc.scalar.activation(Z[:, bass.ds(4 * i + k, 1), half[a]].rearrange("p o t -> p (o t)"),
                                                    bank[:, half[a]], ACT.Copy, scale=g)
                    last.then_inc(emptied[b], 1)
                    if ahead:
                        split_hi(tl.ahead(2))

                for k in range(4):
                    out_tile(0, k, True)
                with act.Fori(1, KT // 4 - 1) as i:
                    for k in range(4):
                        out_tile(i, k, True)
                        if L == 0 and k == 0:
                            ada_columns(late_unit("out", i)[0] - 1, "ada_out", "ac")
                for k in range(4):
                    out_tile(KT // 4 - 1, k, not (L == LAYERS - 1 and k >= 2))
                    if L == 0 and k == 0:
                        ada_columns(LATE - 1, "ada_out", "ac")
                items["ysq"] += KT
                take_root(Q)
                if L < LAYERS - 1:
                    new_squares(LAT)
                    act.dma_start(xback[:, :, :], spill[:, :, 0:CTX]).then_inc(back, 16)
                    take_root(LAT)
                    modulated_hi(LAT)
                    act.wait_ge(back, 16 * (2 * L + 2))
                    act.dma_start(spill[:, :, LAT], Z[:, :, LAT]).then_inc(spilled, 16)
            for g in range(8):
                q, blk = g // 2, g % 2
                b = wait_filled("final", f"o{g}")
                nc.scalar.activation(oout[:, blk, 512 * q:512 * q + 512], ps[b][:, :], ACT.Copy).then_inc(o_ready, 1)

        @block.vector
        def _(dve):
            links = [0]
            step = dict(i=0, per=0, k=0)

            def link(ins):
                step["k"] += 1
                ins.then_inc(dve_chain, 1)
                dve.wait_ge(dve_chain, links[0] + step["k"] + step["per"] * step["i"])

            def begin(i=0, per=0):
                step.update(i=i, per=per, k=0)

            def end(trips=1):
                if step["per"]:
                    assert step["k"] == step["per"], ("links of a step", step["k"])
                links[0] += step["k"] * trips

            def bank_of(key, name):
                b = banks.bank(key, name)
                return b, ps[b]

            def wait_filled(key, name, i=0):
                b = banks.bank(key, name)
                dve.wait_ge(filled[b], banks.filled(key, name, i))
                return b

            def wait_emptied(key, name, i=0):
                b = banks.bank(key, name)
                dve.wait_ge(emptied[b], banks.before(key, name, i) + 1)

            def split_lo(t):
                dve.wait_ge(hi_done, t.n + 1)
                nc.vector.tensor_tensor(wl[:, t.split, :], raw[:, t.raw, :], wh[:, t.split, :].bitcast(F32),
                                        ALU.subtract).then_inc(lo_done, 1)

            begin()
            link(nc.vector.memset(cst[:, :].bitcast(F32), 0.0))
            b = wait_filled("vec", "vt")
            dve.wait_ge(c_exp, 1)
            link(nc.vector.tensor_scalar(tmp[:, 3, 32:64], tmp[:, 3, 0:32], 1.0, None, ALU.add))
            link(nc.vector.reciprocal(tmp[:, 3, 64:96], tmp[:, 3, 32:64]))
            link(nc.vector.tensor_tensor(scol[:, :], ps[b][:, 0:32], tmp[:, 3, 64:96], ALU.mult))
            nc.vector.tensor_copy(bcol[:, :], ps[b][:, P:P + LAYERS * 3 * KT])
            nc.vector.tensor_copy(vcol[:, :], ps[b][:, 0:V_N]).then_inc(emptied[b], 1)
            csv = cst[:, 0:4 * KT].rearrange("p (k e) -> p k e", e=4)
            for s in range(2):
                link(nc.vector.tensor_copy(csv[:, :, 2 * s], scol[:, 16 * s:16 * s + 16]))
                last = nc.vector.tensor_tensor(csv[:, :, 2 * s + 1], scol[:, 16 * s:16 * s + 16],
                                               csv[:, :, 2 * s].bitcast(F32), ALU.subtract)
            last.then_inc(c_ready, 1)
            dve.wait_ge(lam_loaded, 16 * 4 * LAYERS)
            for L in range(LAYERS):
                for t in range(2):
                    last = nc.vector.tensor_tensor_reduce(lamr[:, 4 * L + 2 * t, :], lamr[:, 4 * L + 2 * t, :], lamr[:, 4 * L + 2 * t + 1, :],
                                                          1.0, 0.0, ALU.mult, ALU.add, ldot[:, L, t:t + 1])
                last.then_inc(lam_dot, 1)
            dve.wait_ge(lam_exp, 1)
            for L in range(LAYERS):
                lam_init = 0.8 - 0.6 * math.exp(-0.3 * L)
                link(nc.vector.tensor_tensor(neglam[:, L:L + 1], lexp[:, L, 1:2], lexp[:, L, 0:1], ALU.subtract))
                link(nc.vector.tensor_scalar(neglam[:, L:L + 1], neglam[:, L:L + 1], -lam_init, None, ALU.add))
            end()

            n = dict(root=0, mod=0, c=0, ysq=0, xsq=KT, halfway=0)

            def rstd_of(key, name, width, cols):
                b = banks.bank(key, name)
                nc.vector.tensor_scalar(rs[:, cols], ps[b][:, cols], 1.0 / width, EPS, ALU.mult, ALU.add).then_inc(ms_ready, 1)
                n["root"] += 1
                dve.wait_ge(root_ready, n["root"])
                nc.vector.reciprocal(rs[:, cols], rs[:, cols]).then_inc(emptied[b], 1)
                dve.wait_ge(emptied[b], banks.before(key, name) + 1)

            def ada_step(i, tokens=False):
                for j in range(2):
                    for t in range(4):
                        if tokens:
                            d = 8 * j + 2 * t + 1
                            b = wait_filled("x", f"x{d}")
                            nc.vector.tensor_copy(Z[:, d, :], ps[b][:, :]).then_inc(emptied[b], 1)
                        split_lo(Tile(4 * j + t, i, 8).ahead(2))
                    b = wait_filled("ada", f"col{j}", i)
                    nc.vector.tensor_copy(ada[:, 0, bass.ds(4 * i + KT * j, 4), :],
                                          ps[b][:, 0:8].rearrange("p (u s) -> p u s", s=2)).then_inc(emptied[b], 1)

            split_lo(Tile(0))
            split_lo(Tile(1))
            ada_step(0, True)
            begin()
            dve.wait_ge(sq_used, KT)
            rstd_of("sumx", "ssx0", D, slice(0, TOK))
            end()
            with dve.Fori(1, ADA_FIRST // 2) as i:
                ada_step(i)

            def add_bias(L, c0, c1):
                link(nc.vector.tensor_tensor(ada[:, L, c0:c1, :], ada[:, L, c0:c1, :],
                                             bcol[:, 3 * KT * L + c0:3 * KT * L + c1, None].to_broadcast([P, c1 - c0, 2]), ALU.add))

            def scale_columns(L):
                pre = vcol[:, V_PRE + KT * L:V_PRE + KT * L + KT]
                for s in range(2):
                    last = nc.vector.scalar_tensor_tensor(out=A[:, L, :, s], in0=ada[:, L, KT:2 * KT, s], scalar=1.0, in1=pre,
                                                          op0=ALU.add, op1=ALU.mult)
                return last

            def gate_columns(L):
                post = vcol[:, V_POST + KT * L:V_POST + KT * L + KT]
                for s in range(2):
                    last = nc.vector.tensor_tensor(G[:, L, :, s], ada[:, L, 2 * KT:3 * KT, s], post, ALU.mult)
                return last

            for b in (2, 3):
                dve.wait_ge(emptied[b], banks.before("ada", f"col{b - 2}", ADA_FIRST // 2 - 1) + 1)
            begin()
            dve.wait_ge(emptied[0], 1)
            add_bias(0, 0, 2 * KT)
            for L in range(LAYERS):
                lam_init = 0.8 - 0.6 * math.exp(-0.3 * L)
                nc.vector.tensor_scalar(subc[:, L:L + 1], vcol[:, V_SUB + L:V_SUB + L + 1], 1.0 - lam_init, None, ALU.mult)
            scale_columns(0).then_inc(consts_ready, 1)
            dve.wait_ge(consts_ready, 1)
            end()

            def add_halves(unit, h0, h1):
                number = unit[0]
                for h in range(h0, h1):
                    dve.wait_ge(half_loaded[h % 2], 16 * (4 * number + h // 2 + 1))
                    for kk in range(2):
                        k = 2 * h + kk
                        w = araw[:, h % 2, 512 * kk:512 * kk + 512]
                        for s in range(2):
                            c_k = scol[:, KT * s + k:KT * s + k + 1]
                            if k == 0:
                                if s == 0 and not (isinstance(number, int) and number == 0):
                                    dve.wait_ge(ada_summed, number)
                                nc.vector.tensor_scalar(aacc[:, s, :], w, c_k, None, ALU.mult).then_inc(ada_added, 1)
                            else:
                                dve.wait_ge(ada_added, 32 * number + 2 * k + s - 1)
                                nc.vector.scalar_tensor_tensor(out=aacc[:, s, :], in0=w, scalar=c_k, in1=aacc[:, s, :],
                                                               op0=ALU.mult, op1=ALU.add).then_inc(ada_added, 1)

            def two_steps(first_op, second_op):
                for t in range(KT + 1):
                    if t < KT:
                        first_op(t).then_inc(halfway, 1)
                    if t:
                        n["halfway"] += 1
                        dve.wait_ge(halfway, n["halfway"])
                        second_op(t - 1)

            def modulate(L, cols, halves):
                m0 = n["mod"]
                n["mod"] += KT

                def normed(t):
                    if m0 + t >= 4:
                        dve.wait_ge(hlo, m0 + t - 3)
                    return nc.vector.tensor_tensor(tmp[:, (m0 + t) % 4, cols], Z[:, t, cols], rs[:, cols], ALU.mult)

                def modulated(t):
                    for a in halves:
                        e, v = stream[a], tmp[:, (m0 + t) % 4, half[a]]
                        last = nc.vector.tensor_scalar(v, v, A[:, L, t, e:e + 1], ada[:, L, t, e:e + 1], ALU.mult, ALU.add)
                    last.then_inc(hval, 1)

                two_steps(normed, modulated)

            def new_residual(cols, part):
                dve.wait_ge(back, 16 * part)
                two_steps(lambda t: nc.vector.tensor_tensor(Z[:, t, cols], Z[:, t, cols], rs[:, cols], ALU.mult),
                          lambda t: nc.vector.tensor_tensor(Z[:, t, cols], Z[:, t, cols], xback[:, t, :], ALU.add).then_inc(xnew, 1))

            def rope(key, name, i, bufs, rows):
                b = wait_filled(key, name, i)
                nb = bufs.shape[1]
                src = ps[b][rows, 0:256 * nb].rearrange("p (a t) -> p a t", a=nb)
                t = tmp[rows, 0, 0:256 * nb].rearrange("p (a t) -> p a t", a=nb)
                cs, sn = (v[rows, None, :].to_broadcast([src.shape[0], nb, SEQ]) for v in (cos, sin))
                nc.vector.tensor_tensor(t, src, sn, ALU.mult).then_inc(emptied[b], 1)
                link(nc.vector.tensor_tensor(bufs, bufs, cs, ALU.mult))
                dve.wait_ge(emptied[b], banks.before(key, name, i) + 1)
                nc.vector.tensor_tensor(bufs, bufs, t, ALU.add).then_inc(roped, 1)

            def head(kind, L, i, j, tq, tg, H, y_at, D_no):
                key, s = (kind, L), str(j)
                Q = qcols(L)
                steps = SPREAD[kind][j]

                def late_ada(a):
                    if L == 0:
                        h0 = sum(sum(v) for v in SPREAD[kind][:j]) + sum(steps[:a])
                        add_halves(late_unit(kind, i), h0, h0 + steps[a])

                def values():
                    b = wait_filled(key, "vn" + s, i)
                    nc.vector.tensor_copy(vN[:, :, :], ps[b][:, :].rearrange("p (k d) -> p k d", d=P)).then_inc(emptied[b], 1)

                def maxima(r):
                    for m, name in enumerate(score_names(kind, L, r)):
                        b = wait_filled(key, name + s, i)
                        if r < 2:
                            last = nc.vector.tensor_reduce(nmx[:, m, r, 0:1], ps[b][:, :], AX.X, ALU.max, negate=True)
                        else:
                            last = nc.vector.tensor_reduce(nmx[:, m, r, :], ps[b][:, :].rearrange("p (q k) -> p q k", q=2),
                                                           AX.X, ALU.max, negate=True)
                    last.then_inc(max_done[r], 1)

                def normalise(r):
                    nq = 1 if r < 2 else 2
                    w = TOK // nq
                    names = score_names(kind, L, r)
                    for m, name in enumerate(names):
                        wait_emptied(key, name + s, i)
                    link(nc.vector.reciprocal(rc[:, 0:len(names), r, 0:nq], sm[:, 0:len(names), r, 0:nq]))
                    if kind == "diff":
                        link(nc.vector.tensor_scalar(rc[:, 1, r, 0:nq], rc[:, 1, r, 0:nq], neglam[:, L:L + 1], None, ALU.mult))
                    for t in range(nq):
                        p0 = probs[:, 0, r, w * t:w * t + w]
                        last = nc.vector.tensor_scalar(p0, p0, rc[:, 0, r, t:t + 1], None, ALU.mult)
                    if kind == "diff":
                        link(last)
                        for t in range(nq):
                            p0, p1 = (probs[:, m, r, w * t:w * t + w] for m in (0, 1))
                            last = nc.vector.scalar_tensor_tensor(out=p0, in0=p1, scalar=rc[:, 1, r, t:t + 1], in1=p0,
                                                                  op0=ALU.mult, op1=ALU.add)
                    last.then_inc(norm_done[r], 1)

                if kind == "mla":
                    rope(key, "rot" + s, i, qr[0:64, None, LAT], slice(0, 64))
                    values()
                    split_lo(tq.ahead(2))
                    late_ada(0)
                else:
                    split_lo(tq.ahead(2))
                    late_ada(0)
                    if kind == "diff":
                        rope(key, "rot" + s, i, qk[:, :, LAT], slice(0, P))
                    split_lo(tq.ahead(3))
                    late_ada(1)
                for r in row_groups(L):
                    maxima(r)
                for r in row_groups(L):
                    normalise(r)
                if kind != "mla":
                    values()
                    split_lo(tq.ahead(4))
                    late_ada(2)
                if kind == "diff":
                    b = wait_filled(key, "ss" + s, i)
                    nc.vector.tensor_scalar(rs[:, Q], ps[b][:, Q], 1.0 / P, EPS, ALU.mult, ALU.add).then_inc(emptied[b], 1)
                late_ada(3)
                split_lo(tg.ahead(2))
                wait_emptied(key, "g" + s, i)
                link(nc.vector.tensor_scalar(ge[:, Q], ge[:, Q], 1.0, None, ALU.add))
                if kind == "diff":
                    dve.wait_ge(droot_ready, D_no + 1)
                    link(nc.vector.tensor_tensor(ge[:, Q], ge[:, Q], rs[:, Q], ALU.mult))
                link(nc.vector.reciprocal(ge[:, Q], ge[:, Q]))
                link(nc.vector.tensor_tensor(gs[:, Q], gs[:, Q], ge[:, Q], ALU.mult))
                y = Z[:, y_at, Q].rearrange("p o t -> p (o t)")
                if kind == "diff":
                    b, bank = bank_of(key, "o" + s)
                    nc.vector.scalar_tensor_tensor(out=y, in0=bank[:, Q], scalar=subc[:, L:L + 1], in1=gs[:, Q],
                                                   op0=ALU.mult, op1=ALU.mult).then_inc(emptied[b], 1)
                else:
                    b = wait_filled(key, "o" + s, i)
                    nc.vector.tensor_tensor(y, ps[b][:, Q], gs[:, Q], ALU.mult).then_inc(emptied[b], 1)

            for L in range(LAYERS):
                key = ("pre", L)
                Q = qcols(L)
                begin()

                def ahead(t):
                    split_lo(Tile(first[L] + t + 2))

                def compressed(name, nt, raws, dsth, dstl, v0, then=None):
                    cols = Q if name == "ssq" else slice(0, TOK)
                    n["xsq"] += nt
                    dve.wait_ge(sq_used, n["xsq"])
                    rstd_of(key, name, P * nt, cols)
                    if then is not None:
                        ahead(then)
                    for t in range(nt + 1):
                        if t < nt:
                            nc.vector.scalar_tensor_tensor(out=tmp[:, t, cols], in0=raws[:, t, cols], scalar=vcol[:, v0 + t:v0 + t + 1],
                                                           in1=rs[:, cols], op0=ALU.mult, op1=ALU.mult).then_inc(cnorm, 1)
                        if t:
                            n["c"] += 1
                            dve.wait_ge(chi, n["c"])
                            nc.vector.tensor_tensor(dstl[:, t - 1, cols], tmp[:, t - 1, cols], dsth[:, t - 1, cols].bitcast(F32),
                                                    ALU.subtract).then_inc(clo, 1)
                    dve.wait_ge(clo, n["c"])

                if L == 0:
                    modulate(0, slice(0, TOK), (0, 1))
                    ahead(0)
                    ahead(1)
                    add_halves(late_unit("pre"), 0, 3)
                else:
                    new_residual(slice(0, CTX), 2)
                    ahead(0)
                    ahead(1)
                    n["xsq"] += KT + 1
                    dve.wait_ge(sq_used, n["xsq"])
                    n["xsq"] -= 1
                    rstd_of(key, "ssx1", D, slice(0, CTX))
                    ahead(2)
                    modulate(1, slice(0, CTX), (0,))
                for t in range(2 + L, PRE_TILES - 1):
                    ahead(t)
                    if L == 0 and t < 4:
                        add_halves(late_unit("pre"), 3 * (t - 1), min(3 * t, HALVES))
                    if t == 4:
                        compressed("ssq", 4, cqraw, cqh, cql, V_QN + 4 * L)
                    elif t == 5:
                        compressed("sskv", 2, kvraw, kvh, kvl, V_KVN + 2 * L, t + 1)
                rope(key, "rot", 0, kr[0:64, None, LAT], slice(0, 64))
                dve.wait_ge(roped, ropes * L + 1)
                end()
                i_links = LINKS[("mla", L)]
                with dve.Fori(0, MLA_H // 2) as i:
                    begin(i, i_links)
                    for j in range(2):
                        tq = Tile(mla0[L] + 2 * j, i)
                        head("mla", L, i, j, tq, tq.ahead(1), HEADS * L + j + 2 * i, bass.ds(2 * i + j, 1), None)
                end(MLA_H // 2)
                with dve.Fori(0, NA_H) as i:
                    begin(i, LINKS[("na", L)])
                    tq = Tile(na0[L], i)
                    head("na", L, i, 0, tq, tq.ahead(3), HEADS * L + MLA_H + i, bass.ds(MLA_H + i, 1), None)
                end(NA_H)
                if L == 0:
                    begin()
                    dve.wait_ge(emptied[5], banks.before(("na", 0), "ac0", 0) + 1)
                    add_bias(0, 2 * KT, 3 * KT)
                    gate_columns(0).then_inc(consts_ready, 1)
                    end()
                with dve.Fori(0, DIFF_H) as i:
                    begin(i, LINKS[("diff", L)])
                    tq = Tile(diff0[L], i)
                    head("diff", L, i, 0, tq, tq.ahead(3), HEADS * L + MLA_H + NA_H + i, bass.ds(MLA_H + NA_H + i, 1), DIFF_H * L + i)
                end(DIFF_H)
                for t in range(POOL_HEADS, KT):
                    dve.wait_ge(yhi, L * KT + t + 1)
                    nc.vector.tensor_tensor(hl[:, t, Q], Z[:, t, Q], hh[:, t, Q].bitcast(F32), ALU.subtract).then_inc(ylo, 1)

                def out_tile(i, k, ahead):
                    dve.wait_ge(ysq_ready, n["ysq"] + 4 * i + k + 1)
                    if isinstance(i, int) and i == 0 and k == 0:
                        nc.vector.tensor_copy(acc[:, Q], sq[0][:, Q]).then_inc(acc_ready, 1)
                    else:
                        dve.wait_ge(acc_ready, n["ysq"] + 4 * i + k)
                        nc.vector.tensor_tensor(acc[:, Q], acc[:, Q], sq[k % 2][:, Q], ALU.add).then_inc(acc_ready, 1)
                    if ahead:
                        split_lo(Tile(out0[L] + k, i).ahead(2))

                for k in range(4):
                    out_tile(0, k, True)
                with dve.Fori(1, KT // 4 - 1) as i:
                    for k in range(4):
                        out_tile(i, k, True)
                        if L == 0:
                            h0 = (0, 3, 6, 8)[k]
                            add_halves(late_unit("out", i), h0, (3, 6, 8, 8)[k])
                for k in range(4):
                    out_tile(KT // 4 - 1, k, not (L == LAYERS - 1 and k >= 2))
                n["ysq"] += KT
                begin()
                if L == 0:
                    dve.wait_ge(emptied[5], banks.before("ada_out", "ac", 2) + 1)
                    add_bias(1, 0, 3 * KT)
                    gate_columns(1)
                    scale_columns(1).then_inc(consts_ready, 1)
                    dve.wait_ge(consts_ready, 3)
                b = wait_filled(("post", L), "ssy")
                rstd_of(("post", L), "ssy", D, Q)
                for b in (0, 1):
                    dve.wait_ge(emptied[b], banks.before(("out", L), f"y{2 + b}", KT // 4 - 1) + 1)
                new_residual(LAT, 2 * L + 1)
                if L < LAYERS - 1:
                    n["xsq"] += KT
                    dve.wait_ge(sq_used, n["xsq"])
                    rstd_of(("pre", L + 1), "ssx0", D, LAT)
                    modulate(L + 1, LAT, (1,))
                end()

        @block.tensor
        def _(pe):
            def claim(key, name, i=0):
                b = banks.bank(key, name)
                u = banks.before(key, name, i)
                if not isinstance(u, int) or u > 0:
                    pe.wait_ge(emptied[b], u)
                return b, ps[b]

            def wait_emptied(key, name, i=0):
                b = banks.bank(key, name)
                pe.wait_ge(emptied[b], banks.before(key, name, i) + 1)

            def mm3(out_ap, slot_, c0, cols_w, xh, xl, k, tok, start, stop):
                a, b = wh[:, slot_, c0:c0 + cols_w], wl[:, slot_, c0:c0 + cols_w]
                nc.tensor.matmul(out_ap, a, xh[:, k, tok], start=start, stop=False)
                nc.tensor.matmul(out_ap, a, xl[:, k, tok], start=False, stop=False)
                return nc.tensor.matmul(out_ap, b, xh[:, k, tok], start=False, stop=stop)

            def project(bank, t, tok, k0=0, k1=KT):
                for k in range(k0, k1):
                    last = mm3(bank[:, tok], t.split, P * k, P, hh, hl, k, tok, k == 0, k == KT - 1)
                return last

            pe.wait_ge(tab_loaded, 16)
            pe.wait_ge(vec_loaded, 16 * 8)
            nb = LAYERS * 3 * KT
            nc.tensor.transpose(ps[0][:, P:P + nb], brows[:, :], ident[0:nb, 0:nb])
            nc.tensor.transpose(ps[0][:, 0:V_N], vrows[:, :], ident[0:V_N, 0:V_N]).then_inc(filled[0], 1)
            items = dict(xsq=0)

            def add_squares(bank, cols, first_one, last_one):
                k = items["xsq"]
                pe.wait_ge(xsq_ready, k + 1)
                nc.tensor.matmul(bank[:, cols], ones, sqx[:, k % 3, cols], start=first_one, stop=last_one).then_inc(sq_used, 1)
                items["xsq"] = k + 1

            def turn_tokens(d):
                b, bank = claim("x", f"x{d}")
                for blk in range(4):
                    last = nc.tensor.transpose(bank[:, P * blk:P * blk + P], xin[:, blk, P * d:P * d + P], ident)
                last.then_inc(filled[b], 1)

            def ada_step(i, tokens=False):
                for j in range(2):
                    b, bank = claim("ada", f"row{j}", i)
                    for t in range(4):
                        tl = Tile(4 * j + t, i, 8)
                        if tokens:
                            for d in range(2):
                                turn_tokens(8 * j + 2 * t + d)
                        pe.wait_ge(lo_done, tl.n + 1)
                        for kk in range(4):
                            k = 4 * t + kk
                            st = cst[:, 4 * k:4 * k + P]
                            nc.tensor.matmul(bank[:, :], st, wh[:, tl.split, 512 * kk:512 * kk + 512], start=(k == 0), stop=False)
                            last = nc.tensor.matmul(bank[:, :], st, wl[:, tl.split, 512 * kk:512 * kk + 512], start=False, stop=(k == KT - 1))
                        last.then_inc(tile_used, 1)
                        if tokens and j + t:
                            add_token_squares(8 * j + 2 * t - 2)
                    wait_emptied("ada", f"row{j}", i)
                    b, bank = claim("ada", f"col{j}", i)
                    for u in range(4):
                        last = nc.tensor.matmul(bank[:, 2 * u:2 * u + 2], arow[:, j, P * u:P * u + P], sel, start=True, stop=True)
                    last.then_inc(filled[b], 1)

            def add_token_squares(d0):
                for d in (d0, d0 + 1):
                    add_squares(ps[banks.bank("sumx", "ssx0")], slice(0, TOK), d == 0, d == KT - 1)

            pe.wait_ge(x_loaded, 32)
            pe.wait_ge(c_ready, 1)
            ada_step(0, True)
            add_token_squares(KT - 2)
            with pe.Fori(1, ADA_FIRST // 2) as i:
                ada_step(i)

            def sum_unit(number, key, name, i=0):
                pe.wait_ge(ada_added, 32 * number + 32)
                _, bank = claim(key, name, i)
                for u in range(4):
                    for s in range(2):
                        last = nc.tensor.matmul(bank[:, 2 * u + s:2 * u + s + 1], aacc[:, s, P * u:P * u + P], ones[:, 0:1],
                                                start=True, stop=True)
                last.then_inc(ada_summed, 1)

            def head(kind, L, i, j, tq, tg, H, NA_no, rope_no, D_no):
                key, s = (kind, L), str(j)
                Q = qcols(L)
                allt = slice(0, TOK)
                if kind == "mla":
                    pe.wait_ge(lo_done, tq.n + 1)
                    sl = tq.split
                    for name, c0, nk, xh, xl, tok, step_c in (("qn", 0, 4, cqh, cql, Q, 192), ("qr", 128, 4, cqh, cql, Q, 192),
                                                              ("kn", 768, 2, kvh, kvl, allt, 256), ("v", 768 + 128, 2, kvh, kvl, allt, 256)):
                        if name == "kn":
                            pe.wait_ge(clo, 6 * (L + 1))
                        b, bank = claim(key, name + s, i)
                        for k in range(nk):
                            last = mm3(bank[:, tok], sl, c0 + step_c * k, P, xh, xl, k, tok, k == 0, k == nk - 1)
                        last.then_inc(tile_used if name == "v" else filled[b], 1)
                else:
                    for k, (name, tok) in enumerate((("q", Q), ("k", allt))):
                        tl = tq.ahead(k)
                        pe.wait_ge(lo_done, tl.n + 1)
                        b, bank = claim(key, name + s, i)
                        project(bank, tl, tok).then_inc(tile_used, 1)
                        if L == 0 and k == 0:
                            sum_unit(late_unit(kind, i)[0] - 1, key, "ac0", i)
                    tv = tq.ahead(2)
                    pe.wait_ge(lo_done, tv.n + 1)
                    _, vbank = claim(key, "v" + s, i)
                    project(vbank, tv, allt, 0, 6)

                def gate(k0, k1):
                    if k0 == 0:
                        pe.wait_ge(lo_done, tg.n + 1)
                        claim(key, "g" + s, i)
                    last = project(ps[banks.bank(key, "g" + s)], tg, Q, k0, k1)
                    if k1 == KT:
                        last.then_inc(tile_used, 1)

                def turn_values():
                    wait_emptied(key, "v" + s, i)
                    b, bank = claim(key, "vn" + s, i)
                    for kt in range(4):
                        last = nc.tensor.transpose(bank[:, P * kt:P * kt + P], vT[:, P * kt:P * kt + P], ident)
                    last.then_inc(filled[b], 1)

                if kind == "mla":
                    gate(0, 4)
                    wait_emptied(key, "qr" + s, i)
                    b, bank = claim(key, "rot" + s, i)
                    nc.tensor.matmul(bank[:, 0:256], rotm[0:64, :], qr[0:64, LAT], start=True, stop=True).then_inc(filled[b], 1)
                    if L == 0 and j == 0:
                        sum_unit(late_unit(kind, i)[0] - 1, key, "ac0", i)
                    turn_values()
                    gate(4, 8)
                elif kind == "diff":
                    wait_emptied(key, "q" + s, i)
                    wait_emptied(key, "k" + s, i)
                    b, bank = claim(key, "rot" + s, i)
                    nc.tensor.matmul(bank[:, 0:256], rotm, qk[:, 0, LAT], start=True, stop=True)
                    nc.tensor.matmul(bank[:, 256:512], rotm, qk[:, 1, LAT], start=True, stop=True).then_inc(filled[b], 1)
                if kind != "mla":
                    project(vbank, tv, allt, 6, 12)
                if kind == "na":
                    wait_emptied(key, "q" + s, i)
                    wait_emptied(key, "k" + s, i)
                    pe.wait_ge(bias_built, NA_no + 1)
                elif kind == "mla":
                    wait_emptied(key, "qn" + s, i)
                    wait_emptied(key, "kn" + s, i)
                    pe.wait_ge(roped, rope_no)
                else:
                    pe.wait_ge(roped, rope_no)
                names = [nm for r in row_groups(L) for nm in score_names(kind, L, r)]
                for x_, name in enumerate(names):
                    r = 2 if "ctx" in name else int(name[5])
                    b, bank = claim(key, name + s, i)
                    parts = [(P * 2 + P * r, slice(0, TOK), bank[:, :])] if r < 2 else [
                        (P * t, slice(0, CTX), bank[:, CTX * t:CTX * t + CTX]) for t in range(2)]
                    for q0, keys, dst in parts:
                        if kind == "diff":
                            rows = slice(0, 64) if name[-1] == "a" else slice(64, 128)
                            last = nc.tensor.matmul(dst, qk[rows, 0, q0:q0 + P], qk[rows, 1, keys], start=True, stop=True)
                        elif kind == "mla":
                            nc.tensor.matmul(dst, qk[:, 0, q0:q0 + P], qk[:, 1, keys], start=True, stop=False)
                            last = nc.tensor.matmul(dst, qr[0:64, q0:q0 + P], kr[0:64, keys], start=False, stop=True)
                        elif r < 2:
                            nc.tensor.matmul(dst, qk[:, 0, q0:q0 + P], qk[:, 1, keys], start=True, stop=False)
                            w0 = GRID_W * (2 - 2 * r)
                            last = nc.tensor.matmul(bank[:, LAT], rev, btm[:, w0:w0 + SEQ], start=False, stop=True)
                        else:
                            last = nc.tensor.matmul(dst, qk[:, 0, q0:q0 + P], qk[:, 1, keys], start=True, stop=True)
                    last.then_inc(filled[b], 1)
                    if kind == "diff" and x_ == 2:
                        project(vbank, tv, allt, 12, KT).then_inc(tile_used, 1)
                if kind == "mla":
                    gate(8, 14)
                else:
                    if kind == "na":
                        project(vbank, tv, allt, 12, KT).then_inc(tile_used, 1)
                    gate(0, 4 if kind == "na" else 7)
                    turn_values()
                for r in row_groups(L):
                    pe.wait_ge(norm_done[r], H + 1)
                    b, bank = claim(key, ("pt_lat0", "pt_lat1", "pt_ctx")[r] + s, i)
                    if r < 2:
                        for kt in range(4):
                            last = nc.tensor.transpose(bank[:, P * kt:P * kt + P], probs[:, 0, r, P * kt:P * kt + P], ident)
                    else:
                        for kt in range(2):
                            for t in range(2):
                                last = nc.tensor.transpose(bank[:, CTX * kt + P * t:CTX * kt + P * t + P],
                                                           probs[:, 0, r, CTX * t + P * kt:CTX * t + P * kt + P], ident)
                    last.then_inc(filled[b], 1)
                if kind == "mla":
                    gate(14, KT)
                elif kind == "na":
                    gate(4, 8)
                else:
                    gate(7, 10)
                wait_emptied(key, "vn" + s, i)
                for r in row_groups(L):
                    wait_emptied(key, ("pt_lat0", "pt_lat1", "pt_ctx")[r] + s, i)
                b, bank = claim(key, "o" + s, i)
                if L == 0:
                    for kt in range(2):
                        nc.tensor.matmul(bank[:, 0:CTX], vN[:, kt, :], ptc[:, kt, :], start=(kt == 0), stop=(kt == 1))
                for kt in range(4):
                    last = nc.tensor.matmul(bank[:, LAT], vN[:, kt, :], ptl[:, kt, :], start=(kt == 0), stop=(kt == 3))
                last.then_inc(filled[b], 1)
                if kind == "diff":
                    gate(10, 13)
                    pe.wait_ge(dsq_ready, D_no + 1)
                    b, bank = claim(key, "ss" + s, i)
                    nc.tensor.matmul(bank[:, Q], ones, sq[1][:, Q], start=True, stop=True).then_inc(filled[b], 1)
                    gate(13, KT)
                elif kind == "na":
                    gate(8, KT)

            for L in range(LAYERS):
                key = ("pre", L)
                Q = qcols(L)
                allt = slice(0, TOK)

                def pre_tile(t):
                    tl = Tile(first[L] + t)
                    pe.wait_ge(lo_done, tl.n + 1)
                    b, bank = claim(key, f"t{t}")
                    tok = Q if t < 4 else allt
                    if t == 0 or (L == 1 and t == 4):
                        for k in range(KT):
                            pe.wait_ge(hlo, (KT * L if t == 0 else 2 * KT) + k + 1)
                            last = project(bank, tl, tok, k, k + 1)
                    elif t == PRE_TILES - 1:
                        project(bank, tl, tok, 0, 12)
                        sums(t - 1)
                        last = project(bank, tl, tok, 12, KT)
                    else:
                        last = project(bank, tl, tok)
                    last.then_inc(tile_used, 1)
                    if 0 < t < PRE_TILES - 1:
                        sums(t - 1)
                    if L == 1 and t == 1:
                        _, sbank = claim(key, "ssx1")
                        for k in range(KT):
                            add_squares(sbank, slice(0, CTX), k == 0, k == KT - 1)

                def sums(t):
                    if t < 6:
                        name = "ssq" if t < 4 else "sskv"
                        if t in (0, 4):
                            claim(key, name)
                        add_squares(ps[banks.bank(key, name)], Q if t < 4 else allt, t in (0, 4), t in (3, 5))

                if L == 1:
                    b, bank = claim(key, "ssx0")
                    for k in range(KT):
                        add_squares(bank, LAT, k == 0, k == KT - 1)
                for t in range(PRE_TILES):
                    pre_tile(t)
                wait_emptied(key, "t6")
                b, bank = claim(key, "rot")
                nc.tensor.matmul(bank[:, 0:256], rotm[0:64, :], kr[0:64, LAT], start=True, stop=True).then_inc(filled[b], 1)
                pe.wait_ge(clo, 6 * L + 4)
                with pe.Fori(0, MLA_H // 2) as i:
                    for j in range(2):
                        tq = Tile(mla0[L] + 2 * j, i)
                        head("mla", L, i, j, tq, tq.ahead(1), HEADS * L + j + 2 * i, None, ropes * L + 2 + j + 2 * i, None)
                with pe.Fori(0, NA_H) as i:
                    tq = Tile(na0[L], i)
                    head("na", L, i, 0, tq, tq.ahead(3), HEADS * L + MLA_H + i, NA_H * L + i, None, None)
                with pe.Fori(0, DIFF_H) as i:
                    tq = Tile(diff0[L], i)
                    head("diff", L, i, 0, tq, tq.ahead(3), HEADS * L + MLA_H + NA_H + i, None, ropes * L + MLA_H + 2 + i, DIFF_H * L + i)

                def out_tile(i, k):
                    tl = Tile(out0[L] + k, i)
                    pe.wait_ge(lo_done, tl.n + 1)
                    b, bank = claim(("out", L), f"y{k}", i)
                    if isinstance(i, int) and k == 0:
                        for kk in range(KT):
                            if kk < POOL_HEADS:
                                pe.wait_ge(ylo_pool, L * POOL_HEADS + kk + 1)
                            else:
                                pe.wait_ge(ylo, L * (KT - POOL_HEADS) + kk - POOL_HEADS + 1)
                            last = project(bank, tl, Q, kk, kk + 1)
                    else:
                        last = project(bank, tl, Q)
                    last.then_inc(tile_used, 1)

                for k in range(4):
                    out_tile(0, k)
                with pe.Fori(1, KT // 4 - 1) as i:
                    for k in range(4):
                        out_tile(i, k)
                        if L == 0 and k == 0:
                            sum_unit(late_unit("out", i)[0] - 1, "ada_out", "ac", i - 1)
                for k in range(4):
                    out_tile(KT // 4 - 1, k)
                    if L == 0 and k == 0:
                        sum_unit(LATE - 1, "ada_out", "ac", 2)
                pe.wait_ge(acc_ready, KT * (L + 1))
                b, bank = claim(("post", L), "ssy")
                nc.tensor.matmul(bank[:, Q], ones, acc[:, Q], start=True, stop=True).then_inc(filled[b], 1)
            for g in range(8):
                q, blk = g // 2, g % 2
                b, bank = claim("final", f"o{g}")
                pe.wait_ge(xnew, 2 * KT * (LAYERS - 1) + 4 * q + 4)
                for dd in range(4):
                    t0 = CTX + P * blk
                    last = nc.tensor.transpose(bank[:, P * dd:P * dd + P], Z[:, 4 * q + dd, t0:t0 + P], ident)
                last.then_inc(filled[b], 1)


DIFF_QK = ROT
POOL_HEADS = 6
SPREAD = {"mla": ((2, 0, 0, 2), (2, 0, 0, 2)), "na": ((4, 0, 0, 4),), "diff": ((4, 0, 2, 2),)}
LINKS = {("mla", 0): 14, ("mla", 1): 12, ("na", 0): 6, ("na", 1): 5, ("diff", 0): 14, ("diff", 1): 11}


def ada_src(w_ada, L, quarter, col):
    v = w_ada[L].rearrange("(k p) n -> p k n", p=P)
    return v[:, 4 * quarter:4 * quarter + 4, bass.ds(col, 512)] if not isinstance(col, int) else v[:, 4 * quarter:4 * quarter + 4, col:col + 512]


_INS = ["x", "c", "ctx", "c_ctx", "w_ada", "b_ada", "norm_pre", "norm_post", "w_in", "mla_q_norm", "mla_kv_norm",
        "w_uq", "w_ukv", "na_rpb", "diff_lq1", "diff_lk1", "diff_lq2", "diff_lk2", "diff_subln", "w_out"]
_OUTS = [((1, SEQ, D), "float32")]


def kernel(**inputs):
    import numpy as _np
    import concourse.bacc as _bacc
    from concourse import mybir as _mybir
    from concourse.bass_utils import run_bass_kernel_spmd as _run

    nc = _bacc.Bacc("TRN2", target_bir_lowering=False, num_devices=1)
    arrays = {"in_table_dram": tables()}
    args = [nc.dram_tensor("in_table_dram", (P, T_W), _mybir.dt.float32, kind="ExternalInput").ap()]
    for name in _INS:
        a = _np.ascontiguousarray(inputs[name])
        arrays[f"in_{name}_dram"] = a
        args.append(nc.dram_tensor(f"in_{name}_dram", a.shape, _mybir.dt.from_np(a.dtype), kind="ExternalInput").ap())
    for i, (shape, dtype) in enumerate(_OUTS):
        dt = _mybir.dt.from_np(_np.dtype(dtype))
        args.append(nc.dram_tensor(f"out_{i}_dram", shape, dt, kind="ExternalOutput").ap())
    backbone(nc, *args)
    r = _run(nc, [arrays], core_ids=[0])
    got = tuple(r.results[0][f"out_{i}_dram"] for i in range(len(_OUTS)))
    return got[0]
```
